# Optimizing a Trainium2 kernel written in Bass

```python
import jax, jax.numpy as jnp
from jax import lax
import numpy as np
import math

D_MODEL = 1024
BATCH = 1
SEQ = 1024
DEPTH = 2

GRID_W = 64
N_HEADS = 16
HEAD_DIM = D_MODEL // N_HEADS
NA_ROWS = 8
NA_COLS = 16
NA_QCOLS = NA_COLS
NA_KCOLS = 2 * NA_COLS
GQA_KV_HEADS = 4
GQA_GROUP = N_HEADS // GQA_KV_HEADS
Q_BLOCK = 128
ROPE_THETA = 10000.0
ROPE_PAIRS = HEAD_DIM // 4
N_GROUPS = 4
EXPERTS_PER_GROUP = 8
N_EXPERTS = N_GROUPS * EXPERTS_PER_GROUP
TOP_K = 2
D_EXPERT = D_MODEL // 2
MOE_BLOCK = 128
N_MIXERS = 2
N_NA_LAYERS = (DEPTH + 1) // 2
N_GQA_LAYERS = DEPTH // 2
DEEPNORM_ALPHA = (2 * DEPTH) ** 0.25
DEEPNORM_BETA = (8 * DEPTH) ** -0.25
ADA_INIT = 0.2
LN_EPS = 1e-5
RMS_EPS = 1e-6


def layer_norm(x, g, b):
    xf = x.astype(jnp.float32)
    mu = xf.mean(-1, keepdims=True)
    var = jnp.square(xf - mu).mean(-1, keepdims=True)
    return ((xf - mu) * lax.rsqrt(var + LN_EPS) * g.astype(jnp.float32) + b.astype(jnp.float32)).astype(x.dtype)

def rms_norm(x, g):
    xf = x.astype(jnp.float32)
    ms = jnp.square(xf).mean(-1, keepdims=True)
    return (xf * lax.rsqrt(ms + RMS_EPS) * g.astype(jnp.float32)).astype(x.dtype)

def neighbourhood_attention(q, k, v, rpb):
    B, S, H, hd = q.shape
    rows = S // GRID_W
    kr = min(NA_ROWS, rows)
    r = jnp.arange(rows, dtype=jnp.int32)
    row_start = jnp.clip(r - kr // 2, 0, rows - kr)
    key_rows = row_start[:, None] + jnp.arange(kr, dtype=jnp.int32)[None, :]
    dr = key_rows - r[:, None] + (NA_ROWS - 1)
    qg = q.reshape(B, rows, GRID_W, H, hd)
    kg = k.reshape(B, rows, GRID_W, H, hd)[:, key_rows]
    vg = v.reshape(B, rows, GRID_W, H, hd)[:, key_rows]
    outs = []
    for q0 in range(0, GRID_W, NA_QCOLS):
        b0 = min(max(q0 - NA_COLS // 2, 0), GRID_W - NA_KCOLS)
        qc = q0 + jnp.arange(NA_QCOLS, dtype=jnp.int32)
        kc = b0 + jnp.arange(NA_KCOLS, dtype=jnp.int32)
        win_start = jnp.clip(qc - NA_COLS // 2, 0, GRID_W - NA_COLS)
        valid = (kc[None, :] >= win_start[:, None]) & (kc[None, :] < win_start[:, None] + NA_COLS)
        dc = jnp.clip(kc[None, :] - qc[:, None] + NA_COLS - 1, 0, 2 * NA_COLS - 2)
        bias = rpb[:, dr[:, None, :, None], dc[None, :, None, :]]
        kb = kg[:, :, :, b0:b0 + NA_KCOLS]
        vb = vg[:, :, :, b0:b0 + NA_KCOLS]
        s = jnp.einsum('brqhd,brikhd->bhrqik', qg[:, :, q0:q0 + NA_QCOLS], kb).astype(jnp.float32)
        s = jnp.where(valid[:, None, :], s + bias.astype(jnp.float32), -jnp.inf)
        p = jax.nn.softmax(s.reshape(B, H, rows, NA_QCOLS, kr * NA_KCOLS), axis=-1)
        p = p.reshape(s.shape).astype(v.dtype)
        outs.append(jnp.einsum('bhrqik,brikhd->brqhd', p, vb))
    return jnp.concatenate(outs, axis=2).reshape(B, S, H, hd)

def neighbourhood_mixer(h, w_qkv, rpb, w_o):
    B, S, D = h.shape
    qkv = (h @ w_qkv).reshape(B, S, 3, N_HEADS, HEAD_DIM)
    q = qkv[:, :, 0] * (HEAD_DIM ** -0.5)
    o = neighbourhood_attention(q, qkv[:, :, 1], qkv[:, :, 2], rpb)
    return o.reshape(B, S, D) @ w_o

def axial_rope_tables(S):
    t = jnp.arange(S, dtype=jnp.int32)
    pos = jnp.stack([t // GRID_W, t % GRID_W], axis=-1).astype(jnp.float32)
    inv_freq = ROPE_THETA ** (-jnp.arange(ROPE_PAIRS, dtype=jnp.float32) / ROPE_PAIRS)
    ang = pos[:, :, None] * inv_freq
    return jnp.cos(ang), jnp.sin(ang)

def apply_axial_rope(x, cos, sin):
    B, S, H, hd = x.shape
    xr = x.astype(jnp.float32).reshape(B, S, H, 2, 2, ROPE_PAIRS)
    x1, x2 = xr[..., 0, :], xr[..., 1, :]
    c, s = cos[None, :, None], sin[None, :, None]
    out = jnp.stack([x1 * c - x2 * s, x2 * c + x1 * s], axis=-2)
    return out.reshape(B, S, H, hd).astype(x.dtype)

def block_gqa_attention(q, k, v):
    B, S, H, hd = q.shape
    nblk = S // Q_BLOCK
    qg = q.reshape(B, nblk, Q_BLOCK, GQA_KV_HEADS, GQA_GROUP, hd).transpose(1, 0, 2, 3, 4, 5)
    scale = HEAD_DIM ** -0.5

    def one_block(qb):
        s = jnp.einsum('bqkgd,bskd->bkgqs', qb, k).astype(jnp.float32) * scale
        p = jax.nn.softmax(s, axis=-1).astype(v.dtype)
        return jnp.einsum('bkgqs,bskd->bqkgd', p, v)

    o = lax.map(one_block, qg)
    return o.transpose(1, 0, 2, 3, 4, 5).reshape(B, S, H * hd)

def gqa_mixer(h, cos, sin, w_qkv, q_gain, k_gain, w_o):
    B, S, D = h.shape
    kvd = GQA_KV_HEADS * HEAD_DIM
    qkv = h @ w_qkv
    q = qkv[..., :D].reshape(B, S, N_HEADS, HEAD_DIM)
    k = qkv[..., D:D + kvd].reshape(B, S, GQA_KV_HEADS, HEAD_DIM)
    v = qkv[..., D + kvd:].reshape(B, S, GQA_KV_HEADS, HEAD_DIM)
    q = apply_axial_rope(rms_norm(q, q_gain), cos, sin)
    k = apply_axial_rope(rms_norm(k, k_gain), cos, sin)
    return block_gqa_attention(q, k, v) @ w_o

def hierarchical_moe(h, w_group, b_group, w_expert, b_expert, w_gate, w_up, w_down):
    B, S, D = h.shape
    N = B * S
    xt = h.reshape(N, D)
    pg = jax.nn.softmax((xt @ w_group).astype(jnp.float32) + b_group.astype(jnp.float32), axis=-1)
    g_prob, g_idx = lax.top_k(pg, 1)
    le = ((xt @ w_expert).astype(jnp.float32) + b_expert.astype(jnp.float32)).reshape(N, N_GROUPS, EXPERTS_PER_GROUP)
    le = le[jnp.arange(N), g_idx[:, 0]]
    e_prob, e_local = lax.top_k(jax.nn.softmax(le, axis=-1), TOP_K)
    e_prob = e_prob / e_prob.sum(-1, keepdims=True)
    gates = g_prob * e_prob
    experts = g_idx * EXPERTS_PER_GROUP + e_local
    A = N * TOP_K
    flat_e = experts.reshape(A).astype(jnp.int32)
    flat_tok = jnp.repeat(jnp.arange(N, dtype=jnp.int32), TOP_K)
    flat_gate = gates.reshape(A)
    order = jnp.argsort(flat_e)
    e_sorted = flat_e[order]
    counts = jnp.bincount(flat_e, length=N_EXPERTS).astype(jnp.int32)
    padded = (counts + MOE_BLOCK - 1) // MOE_BLOCK * MOE_BLOCK
    pad_end = jnp.cumsum(padded)
    pad_start = pad_end - padded
    seg_start = jnp.cumsum(counts) - counts
    dest = pad_start[e_sorted] + (jnp.arange(A, dtype=jnp.int32) - seg_start[e_sorted])
    n_blocks = -(-A // MOE_BLOCK) + N_EXPERTS
    n_rows = n_blocks * MOE_BLOCK
    row_tok = jnp.full((n_rows,), N, jnp.int32).at[dest].set(flat_tok[order])
    row_gate = jnp.zeros((n_rows,), jnp.float32).at[dest].set(flat_gate[order])
    block_expert = jnp.minimum(
        jnp.searchsorted(pad_end, jnp.arange(n_blocks, dtype=jnp.int32) * MOE_BLOCK, side='right'),
        N_EXPERTS - 1)
    x_pad = jnp.concatenate([xt, jnp.zeros((1, D), xt.dtype)], axis=0)
    xs = x_pad[row_tok].reshape(n_blocks, MOE_BLOCK, D)

    def expert_block(args):
        xb, e = args
        return (jax.nn.silu(xb @ w_gate[e]) * (xb @ w_up[e])) @ w_down[e]

    ys = lax.map(expert_block, (xs, block_expert)).reshape(n_rows, D)
    ys = ys * row_gate[:, None].astype(ys.dtype)
    out = jnp.zeros((N + 1, D), ys.dtype).at[row_tok].add(ys)[:N]
    return out.reshape(B, S, D)

def first_inputs(seed: int = 0) -> dict:
    key = jax.random.key(seed)
    ks = jax.random.split(key, 20)
    f32 = jnp.float32
    D = D_MODEL
    inv = D ** -0.5
    kvd = GQA_KV_HEADS * HEAD_DIM

    def nrm(k, shape, scale):
        return jax.random.normal(k, shape, f32) * scale

    na_cols = jnp.concatenate([jnp.ones((2 * D,), f32), jnp.full((D,), DEEPNORM_BETA, f32)])
    gqa_cols = jnp.concatenate([jnp.ones((D + kvd,), f32), jnp.full((kvd,), DEEPNORM_BETA, f32)])
    return {
        "x": nrm(ks[0], (BATCH, SEQ, D), 1.0),
        "c": nrm(ks[1], (BATCH, D), 1.0),
        "ada_w": nrm(ks[2], (DEPTH, D, 6 * D), ADA_INIT * inv),
        "ada_b": nrm(ks[3], (DEPTH, 6 * D), 0.01),
        "ln_g": 1.0 + nrm(ks[4], (DEPTH, 2, D), 0.01),
        "ln_b": nrm(ks[5], (DEPTH, 2, D), 0.01),
        "na_w_qkv": nrm(ks[6], (N_NA_LAYERS, D, 3 * D), inv) * na_cols,
        "na_rpb": nrm(ks[7], (N_NA_LAYERS, N_HEADS, 2 * NA_ROWS - 1, 2 * NA_COLS - 1), 0.1),
        "na_w_o": nrm(ks[8], (N_NA_LAYERS, D, D), inv * DEEPNORM_BETA),
        "gqa_w_qkv": nrm(ks[9], (N_GQA_LAYERS, D, D + 2 * kvd), inv) * gqa_cols,
        "gqa_q_norm": 1.0 + nrm(ks[10], (N_GQA_LAYERS, HEAD_DIM), 0.01),
        "gqa_k_norm": 1.0 + nrm(ks[11], (N_GQA_LAYERS, HEAD_DIM), 0.01),
        "gqa_w_o": nrm(ks[12], (N_GQA_LAYERS, D, D), inv * DEEPNORM_BETA),
        "moe_w_group": nrm(ks[13], (DEPTH, D, N_GROUPS), inv),
        "moe_b_group": nrm(ks[14], (DEPTH, N_GROUPS), 0.01),
        "moe_w_expert": nrm(ks[15], (DEPTH, D, N_EXPERTS), inv),
        "moe_b_expert": nrm(ks[16], (DEPTH, N_EXPERTS), 0.01),
        "moe_w_gate": nrm(ks[17], (DEPTH, N_EXPERTS, D, D_EXPERT), inv),
        "moe_w_up": nrm(ks[18], (DEPTH, N_EXPERTS, D, D_EXPERT), inv),
        "moe_w_down": nrm(ks[19], (DEPTH, N_EXPERTS, D_EXPERT, D), (D_EXPERT ** -0.5) * DEEPNORM_BETA),
    }

def first_block(x, c, ada_w, ada_b, ln_g, ln_b, na_w_qkv, na_rpb, na_w_o, gqa_w_qkv, gqa_q_norm,
              gqa_k_norm, gqa_w_o, moe_w_group, moe_b_group, moe_w_expert, moe_b_expert,
              moe_w_gate, moe_w_up, moe_w_down):
    B, S, D = x.shape
    cos, sin = axial_rope_tables(S)
    c_act = jax.nn.silu(c)
    for i in range(DEPTH):
        mod = c_act @ ada_w[i] + ada_b[i]
        sh1, sc1, g1, sh2, sc2, g2 = jnp.split(mod[:, None, :], 6, axis=-1)
        h = x * (1 + sc1) + sh1
        j = i // N_MIXERS
        if i % N_MIXERS == 0:
            y = neighbourhood_mixer(h, na_w_qkv[j], na_rpb[j], na_w_o[j])
        else:
            y = gqa_mixer(h, cos, sin, gqa_w_qkv[j], gqa_q_norm[j], gqa_k_norm[j], gqa_w_o[j])
        x = layer_norm(DEEPNORM_ALPHA * x + (1 + g1) * y, ln_g[i, 0], ln_b[i, 0])
        h = x * (1 + sc2) + sh2
        y = hierarchical_moe(h, moe_w_group[i], moe_b_group[i], moe_w_expert[i], moe_b_expert[i],
                             moe_w_gate[i], moe_w_up[i], moe_w_down[i])
        x = layer_norm(DEEPNORM_ALPHA * x + (1 + g2) * y, ln_g[i, 1], ln_b[i, 1])
    return x


DEPTH_2 = 1

CHUNK = 64
MLA_WIDTH = D_MODEL // 2
MLA_V_DIM = 64
MLA_HEADS = MLA_WIDTH // MLA_V_DIM
MLA_QK_NOPE = 64
MLA_QK_ROPE = 32
MLA_Q_RANK = D_MODEL // 4
MLA_KV_RANK = D_MODEL // 8
GDN_WIDTH = D_MODEL // 4
GDN_HEAD_DIM = 64
GDN_HEADS = GDN_WIDTH // GDN_HEAD_DIM
GDN_CONV = 4
POOL_WIDTH = D_MODEL - MLA_WIDTH - GDN_WIDTH
POOL_WINDOWS = (2, 4, 8, 16)
POOL_GROUPS = 4
POOL_GROUP_DIM = POOL_WIDTH // POOL_GROUPS
MIX_WIDTH = MLA_WIDTH + GDN_WIDTH + POOL_WIDTH
IN_SIZES = (MLA_Q_RANK, MLA_KV_RANK, MLA_QK_ROPE, GDN_WIDTH, GDN_WIDTH, GDN_WIDTH, GDN_WIDTH, GDN_HEADS, GDN_HEADS, POOL_WIDTH)
IN_PROJ_DIM = sum(IN_SIZES)
N_EXPERTS_2 = N_GROUPS * EXPERTS_PER_GROUP
EXPERT_FF = D_MODEL // 4
DEEPNORM_ALPHA_2 = (2 * DEPTH_2) ** 0.25
DEEPNORM_BETA_2 = (8 * DEPTH_2) ** -0.25


F32 = jnp.float32

def layer_norm_2(x, g, b):
    xf = x.astype(F32)
    mu = jnp.mean(xf, axis=-1, keepdims=True)
    var = jnp.mean(jnp.square(xf - mu), axis=-1, keepdims=True)
    return ((xf - mu) * lax.rsqrt(var + LN_EPS)).astype(x.dtype) * g + b

def rms_norm_2(x, g):
    xf = x.astype(F32)
    return (xf * lax.rsqrt(jnp.mean(xf * xf, axis=-1, keepdims=True) + RMS_EPS)).astype(x.dtype) * g

def l2_norm(x):
    xf = x.astype(F32)
    return xf * lax.rsqrt(jnp.sum(xf * xf, axis=-1, keepdims=True) + RMS_EPS)

def split_sizes(x, sizes):
    offs, acc = [], 0
    for s in sizes[:-1]:
        acc += s
        offs.append(acc)
    return jnp.split(x, offs, axis=-1)

def rope_tables(seq):
    inv_freq = jnp.power(ROPE_THETA, -jnp.arange(0, MLA_QK_ROPE, 2, dtype=F32) / MLA_QK_ROPE)
    ang = jnp.arange(seq, dtype=F32)[:, None] * inv_freq[None, :]
    return jnp.cos(ang), jnp.sin(ang)

def apply_rope(x, cos, sin):
    xf = x.astype(F32)
    x1, x2 = jnp.split(xf, 2, axis=-1)
    return jnp.concatenate([x1 * cos - x2 * sin, x2 * cos + x1 * sin], axis=-1).astype(x.dtype)

def mla_attention(c_q, c_kv, k_rope, q_norm_g, kv_norm_g, w_uq, w_ukv, cos, sin):
    B, S, _ = c_q.shape
    q = (rms_norm_2(c_q, q_norm_g) @ w_uq).reshape(B, S, MLA_HEADS, MLA_QK_NOPE + MLA_QK_ROPE)
    q_nope, q_rope = q[..., :MLA_QK_NOPE], q[..., MLA_QK_NOPE:]
    q_rope = apply_rope(q_rope, cos[:, None, :], sin[:, None, :])
    kv = (rms_norm_2(c_kv, kv_norm_g) @ w_ukv).reshape(B, S, MLA_HEADS, MLA_QK_NOPE + MLA_V_DIM)
    k_nope, v = kv[..., :MLA_QK_NOPE], kv[..., MLA_QK_NOPE:]
    k_rope = apply_rope(k_rope, cos, sin)
    scale = (MLA_QK_NOPE + MLA_QK_ROPE) ** -0.5
    outs = []
    for qb in range(S // Q_BLOCK):
        q0, kend = qb * Q_BLOCK, (qb + 1) * Q_BLOCK
        s = (jnp.einsum('bqhd,bkhd->bhqk', q_nope[:, q0:kend], k_nope[:, :kend])
             + jnp.einsum('bqhd,bkd->bhqk', q_rope[:, q0:kend], k_rope[:, :kend]))
        s = s.astype(F32) * scale
        q_chunk = jnp.arange(q0, kend) // CHUNK
        k_chunk = jnp.arange(kend) // CHUNK
        allowed = k_chunk[None, :] <= q_chunk[:, None]
        p = jax.nn.softmax(jnp.where(allowed, s, -jnp.inf), axis=-1).astype(v.dtype)
        outs.append(jnp.einsum('bhqk,bkhd->bqhd', p, v[:, :kend]))
    return jnp.concatenate(outs, axis=1).reshape(B, S, MLA_WIDTH)

def causal_depthwise_conv(x, w):
    C = x.shape[-1]
    return lax.conv_general_dilated(x, w[:, None, :].astype(x.dtype), window_strides=(1,),
                                    padding=[(GDN_CONV - 1, 0)],
                                    dimension_numbers=('NWC', 'WIO', 'NWC'),
                                    feature_group_count=C)

def gated_delta_rule(q, k, v, g, beta):
    B, S, H, dk = q.shape
    dv = v.shape[-1]
    nc = S // CHUNK

    def to_chunks(t):
        t = t.astype(F32).reshape((B, nc, CHUNK, H) + t.shape[3:])
        return jnp.moveaxis(t, 3, 1)

    qc = to_chunks(q) * dk ** -0.5
    kc, vc = to_chunks(k), to_chunks(v)
    gc = jnp.cumsum(to_chunks(g), axis=-1)
    bc = to_chunks(beta)
    idx = jnp.arange(CHUNK)
    incl = idx[:, None] >= idx[None, :]
    strict = idx[:, None] > idx[None, :]
    diff = gc[..., :, None] - gc[..., None, :]
    decay = jnp.where(incl, jnp.exp(jnp.where(incl, diff, 0.0)), 0.0)
    kb = kc * bc[..., None]
    a_mat = jnp.where(strict, jnp.einsum('bhnid,bhnjd->bhnij', kb, kc) * decay, 0.0)
    lower = a_mat + jnp.eye(CHUNK, dtype=F32)
    rhs = jnp.concatenate([vc * bc[..., None], kb * jnp.exp(gc)[..., None]], axis=-1)
    sol = lax.linalg.triangular_solve(lower, rhs, left_side=True, lower=True, unit_diagonal=True)
    u, w = sol[..., :dv], sol[..., dv:]
    qk = jnp.where(incl, jnp.einsum('bhnid,bhnjd->bhnij', qc, kc) * decay, 0.0)
    q_dec = qc * jnp.exp(gc)[..., None]
    k_dec = kc * jnp.exp(gc[..., -1:] - gc)[..., None]
    g_last = jnp.exp(gc[..., -1])

    def step(state, inp):
        q_i, k_i, u_i, w_i, qk_i, gl_i = inp
        v_new = u_i - jnp.einsum('bhck,bhkv->bhcv', w_i, state)
        o_i = jnp.einsum('bhck,bhkv->bhcv', q_i, state) + jnp.einsum('bhij,bhjv->bhiv', qk_i, v_new)
        state = state * gl_i[..., None, None] + jnp.einsum('bhck,bhcv->bhkv', k_i, v_new)
        return state, o_i

    xs = tuple(jnp.moveaxis(t, 2, 0) for t in (q_dec, k_dec, u, w, qk, g_last))
    _, o = lax.scan(step, jnp.zeros((B, H, dk, dv), F32), xs)
    o = jnp.moveaxis(o, 0, 2).reshape(B, H, S, dv)
    return jnp.transpose(o, (0, 2, 1, 3))

def gdn_mixer(q, k, v, z, a, b, conv_w, a_log, dt_bias, out_g):
    B, S, _ = q.shape
    qkv = jax.nn.silu(causal_depthwise_conv(jnp.concatenate([q, k, v], axis=-1), conv_w))
    q, k, v = jnp.split(qkv, 3, axis=-1)
    shp = (B, S, GDN_HEADS, GDN_HEAD_DIM)
    q, k, v = l2_norm(q.reshape(shp)), l2_norm(k.reshape(shp)), v.reshape(shp)
    g = -jnp.exp(a_log.astype(F32)) * jax.nn.softplus(a.astype(F32) + dt_bias.astype(F32))
    beta = jax.nn.sigmoid(b.astype(F32))
    o = gated_delta_rule(q, k, v, g, beta).astype(z.dtype)
    o = rms_norm_2(o, out_g) * jax.nn.silu(z.reshape(shp))
    return o.reshape(B, S, GDN_WIDTH)

def pool_mixer(p, pool_w, pool_scale):
    B, S, _ = p.shape
    pg = p.reshape(B, S, POOL_GROUPS, POOL_GROUP_DIM).astype(F32)
    cs = jnp.cumsum(pg, axis=1)
    cs = jnp.concatenate([jnp.zeros_like(cs[:, :1]), cs], axis=1)
    t = jnp.arange(S)
    means = []
    for gi, win in enumerate(POOL_WINDOWS):
        start = jnp.maximum(t + 1 - win, 0)
        cnt = (t + 1 - start).astype(F32)
        cs_g = cs[:, :, gi, :]
        means.append((cs_g[:, 1:] - cs_g[:, start]) / cnt[None, :, None])
    delta = (jnp.stack(means, axis=2) - pg).astype(p.dtype)
    mixed = jnp.einsum('bsgc,gcd->bsgd', delta, pool_w)
    return mixed.reshape(B, S, POOL_WIDTH) * pool_scale

def hybrid_mixer(h, w_in, q_norm_g, kv_norm_g, w_uq, w_ukv, conv_w, a_log, dt_bias, gdn_g,
                 pool_w, pool_scale, w_out, cos, sin):
    proj = h @ w_in
    c_q, c_kv, k_rope, gq, gk, gv, gz, ga, gb, p = split_sizes(proj, IN_SIZES)
    y_mla = mla_attention(c_q, c_kv, k_rope, q_norm_g, kv_norm_g, w_uq, w_ukv, cos, sin)
    y_gdn = gdn_mixer(gq, gk, gv, gz, ga, gb, conv_w, a_log, dt_bias, gdn_g)
    y_pool = pool_mixer(p, pool_w, pool_scale)
    return jnp.concatenate([y_mla, y_gdn, y_pool], axis=-1) @ w_out

def grouped_expert_ffn(hf, expert, weights, w_gate, w_up, w_down):
    T, D = hf.shape
    A = T * TOP_K
    flat_e = expert.reshape(A)
    flat_tok = jnp.arange(A, dtype=jnp.int32) // TOP_K
    flat_w = weights.reshape(A).astype(hf.dtype)
    order = jnp.argsort(flat_e)
    se = flat_e[order]
    counts = jax.ops.segment_sum(jnp.ones((A,), jnp.int32), flat_e, num_segments=N_EXPERTS_2)
    padded = (counts + MOE_BLOCK - 1) // MOE_BLOCK * MOE_BLOCK
    pad_end = jnp.cumsum(padded)
    pad_start = pad_end - padded
    start = jnp.cumsum(counts) - counts
    dest = pad_start[se] + (jnp.arange(A, dtype=jnp.int32) - start[se])
    nb = (A + N_EXPERTS_2 * (MOE_BLOCK - 1) + MOE_BLOCK - 1) // MOE_BLOCK
    P = nb * MOE_BLOCK
    buf_tok = jnp.full((P,), T, jnp.int32).at[dest].set(flat_tok[order])
    buf_w = jnp.zeros((P,), hf.dtype).at[dest].set(flat_w[order])
    block_expert = jnp.clip(jnp.searchsorted(pad_end, jnp.arange(nb) * MOE_BLOCK, side='right'), 0, N_EXPERTS_2 - 1)
    xpad = jnp.concatenate([hf, jnp.zeros((1, D), hf.dtype)], axis=0)
    xb = xpad[buf_tok].reshape(nb, MOE_BLOCK, D)

    def block_ffn(args):
        xb_i, e = args
        return (jax.nn.silu(xb_i @ w_gate[e]) * (xb_i @ w_up[e])) @ w_down[e]

    yb = lax.map(block_ffn, (xb, block_expert)).reshape(P, D)
    out = jnp.zeros((T + 1, D), yb.dtype).at[buf_tok].add(yb * buf_w[:, None])
    return out[:T]

def hierarchical_moe_2(h, w_rg, b_rg, w_re, b_re, w_gate, w_up, w_down):
    B, S, D = h.shape
    hf = h.reshape(B * S, D)
    g_prob = jax.nn.softmax((hf @ w_rg + b_rg).astype(F32), axis=-1)
    g_p, g_sel = lax.top_k(g_prob, 1)
    e_logit = (hf @ w_re + b_re).astype(F32).reshape(-1, N_GROUPS, EXPERTS_PER_GROUP)
    e_logit = jnp.take_along_axis(e_logit, g_sel[:, :, None], axis=1)[:, 0]
    e_p, e_idx = lax.top_k(jax.nn.softmax(e_logit, axis=-1), TOP_K)
    weights = g_p * e_p / jnp.sum(e_p, axis=-1, keepdims=True)
    expert = g_sel * EXPERTS_PER_GROUP + e_idx
    return grouped_expert_ffn(hf, expert, weights, w_gate, w_up, w_down).reshape(B, S, D)

def second_inputs(seed: int = 0) -> dict:
    key = jax.random.key(seed)
    ks = jax.random.split(key, 32)
    L, D = DEPTH_2, D_MODEL

    def nrm(k, shape, scale):
        return jax.random.normal(k, shape, F32) * scale

    dt = jnp.exp(jax.random.uniform(ks[9], (L, GDN_HEADS), F32, math.log(1e-3), math.log(1e-1)))
    return {
        'x': nrm(ks[0], (BATCH, SEQ, D), 1.0),
        'c': nrm(ks[1], (BATCH, D), 1.0),
        'w_in': nrm(ks[2], (L, D, IN_PROJ_DIM), D ** -0.5),
        'mla_q_norm': 1.0 + nrm(ks[3], (L, MLA_Q_RANK), 0.05),
        'mla_kv_norm': 1.0 + nrm(ks[4], (L, MLA_KV_RANK), 0.05),
        'mla_w_uq': nrm(ks[5], (L, MLA_Q_RANK, MLA_HEADS * (MLA_QK_NOPE + MLA_QK_ROPE)), MLA_Q_RANK ** -0.5),
        'mla_w_ukv': nrm(ks[6], (L, MLA_KV_RANK, MLA_HEADS * (MLA_QK_NOPE + MLA_V_DIM)), MLA_KV_RANK ** -0.5),
        'gdn_conv': nrm(ks[7], (L, GDN_CONV, 3 * GDN_WIDTH), GDN_CONV ** -0.5),
        'gdn_a_log': jnp.log(jax.random.uniform(ks[8], (L, GDN_HEADS), F32, 1.0, 16.0)),
        'gdn_dt_bias': dt + jnp.log(-jnp.expm1(-dt)),
        'gdn_out_norm': 1.0 + nrm(ks[10], (L, GDN_HEAD_DIM), 0.05),
        'pool_w': nrm(ks[11], (L, POOL_GROUPS, POOL_GROUP_DIM, POOL_GROUP_DIM), POOL_GROUP_DIM ** -0.5),
        'pool_scale': 1.0 + nrm(ks[12], (L, POOL_WIDTH), 0.05),
        'w_out': nrm(ks[13], (L, MIX_WIDTH, D), MIX_WIDTH ** -0.5 * DEEPNORM_BETA_2),
        'w_mod': nrm(ks[14], (L, D, 6 * D), 0.2 * D ** -0.5),
        'b_mod': nrm(ks[15], (L, 6 * D), 0.02),
        'ln1_g': 1.0 + nrm(ks[16], (L, D), 0.05),
        'ln1_b': nrm(ks[17], (L, D), 0.02),
        'ln2_g': 1.0 + nrm(ks[18], (L, D), 0.05),
        'ln2_b': nrm(ks[19], (L, D), 0.02),
        'router_w_group': nrm(ks[20], (L, D, N_GROUPS), D ** -0.5),
        'router_b_group': nrm(ks[21], (L, N_GROUPS), 0.01),
        'router_w_expert': nrm(ks[22], (L, D, N_EXPERTS_2), D ** -0.5),
        'router_b_expert': nrm(ks[23], (L, N_EXPERTS_2), 0.01),
        'moe_w_gate': nrm(ks[24], (L, N_EXPERTS_2, D, EXPERT_FF), D ** -0.5),
        'moe_w_up': nrm(ks[25], (L, N_EXPERTS_2, D, EXPERT_FF), D ** -0.5),
        'moe_w_down': nrm(ks[26], (L, N_EXPERTS_2, EXPERT_FF, D), EXPERT_FF ** -0.5 * DEEPNORM_BETA_2),
    }

def second_block(x, c, w_in, mla_q_norm, mla_kv_norm, mla_w_uq, mla_w_ukv, gdn_conv, gdn_a_log,
              gdn_dt_bias, gdn_out_norm, pool_w, pool_scale, w_out, w_mod, b_mod, ln1_g, ln1_b,
              ln2_g, ln2_b, router_w_group, router_b_group, router_w_expert, router_b_expert,
              moe_w_gate, moe_w_up, moe_w_down):
    cos, sin = rope_tables(x.shape[1])
    c_act = jax.nn.silu(c)
    for l in range(DEPTH_2):
        mod = c_act @ w_mod[l] + b_mod[l]
        sh1, sc1, gt1, sh2, sc2, gt2 = [m[:, None, :] for m in jnp.split(mod, 6, axis=-1)]
        h = x * (1.0 + sc1) + sh1
        y = hybrid_mixer(h, w_in[l], mla_q_norm[l], mla_kv_norm[l], mla_w_uq[l], mla_w_ukv[l],
                         gdn_conv[l], gdn_a_log[l], gdn_dt_bias[l], gdn_out_norm[l],
                         pool_w[l], pool_scale[l], w_out[l], cos, sin)
        x = layer_norm_2(DEEPNORM_ALPHA_2 * x + (1.0 + gt1) * y, ln1_g[l], ln1_b[l])
        h = x * (1.0 + sc2) + sh2
        y = hierarchical_moe_2(h, router_w_group[l], router_b_group[l], router_w_expert[l],
                             router_b_expert[l], moe_w_gate[l], moe_w_up[l], moe_w_down[l])
        x = layer_norm_2(DEEPNORM_ALPHA_2 * x + (1.0 + gt2) * y, ln2_g[l], ln2_b[l])
    return x


def setup_inputs(seed=0):
    out = dict(first_inputs(seed))
    for name, value in second_inputs(seed + 1).items():
        if name != "x":
            out[name + "_2"] = value
    return out


def reference(
    x, c, ada_w, ada_b, ln_g, ln_b, na_w_qkv, na_rpb, na_w_o, gqa_w_qkv, gqa_q_norm, gqa_k_norm,
    gqa_w_o, moe_w_group, moe_b_group, moe_w_expert, moe_b_expert, moe_w_gate, moe_w_up,
    moe_w_down, c_2, w_in_2, mla_q_norm_2, mla_kv_norm_2, mla_w_uq_2, mla_w_ukv_2, gdn_conv_2,
    gdn_a_log_2, gdn_dt_bias_2, gdn_out_norm_2, pool_w_2, pool_scale_2, w_out_2, w_mod_2,
    b_mod_2, ln1_g_2, ln1_b_2, ln2_g_2, ln2_b_2, router_w_group_2, router_b_group_2,
    router_w_expert_2, router_b_expert_2, moe_w_gate_2, moe_w_up_2, moe_w_down_2,
):
    x = first_block(
        x, c, ada_w, ada_b, ln_g, ln_b, na_w_qkv, na_rpb, na_w_o, gqa_w_qkv, gqa_q_norm,
        gqa_k_norm, gqa_w_o, moe_w_group, moe_b_group, moe_w_expert, moe_b_expert, moe_w_gate,
        moe_w_up, moe_w_down,
    )
    return second_block(
        x, c_2, w_in_2, mla_q_norm_2, mla_kv_norm_2, mla_w_uq_2, mla_w_ukv_2, gdn_conv_2,
        gdn_a_log_2, gdn_dt_bias_2, gdn_out_norm_2, pool_w_2, pool_scale_2, w_out_2, w_mod_2,
        b_mod_2, ln1_g_2, ln1_b_2, ln2_g_2, ln2_b_2, router_w_group_2, router_b_group_2,
        router_w_expert_2, router_b_expert_2, moe_w_gate_2, moe_w_up_2, moe_w_down_2,
    )


_drawn_inputs = setup_inputs


def setup_inputs(seed=0):
    import zlib

    import numpy as np

    out = dict(_drawn_inputs(seed))
    spreads = {}
    factors = {'ada_b': 3.514,
     'na_rpb': 5.571,
     'gqa_q_norm': 8.0,
     'gqa_k_norm': 8.0,
     'moe_b_group': 5.332,
     'moe_b_expert': 4.68,
     'mla_q_norm_2': 8.0,
     'mla_kv_norm_2': 7.638,
     'gdn_a_log_2': 3.067,
     'gdn_out_norm_2': 19.689,
     'pool_scale_2': 10.57,
     'router_b_group_2': 28.07,
     'router_b_expert_2': 6.434}
    for name, (base, spread) in spreads.items():
        noise = np.random.default_rng([zlib.crc32(name.encode()), seed]).standard_normal(out[name].shape)
        drawn = base * np.exp(spread * noise) if base else spread * noise
        out[name] = __import__('jax').numpy.asarray(drawn.astype(out[name].dtype))
    for name, factor in factors.items():
        out[name] = (out[name] * factor).astype(out[name].dtype)
    return out
```

```python
from contextlib import ExitStack

import numpy as np
import concourse.bass as bass
from concourse import mybir

P = 128
F32 = mybir.dt.float32
I32 = mybir.dt.int32
U32 = mybir.dt.uint32
ALU = mybir.AluOpType
ACT = mybir.ActivationFunctionType
AX = mybir.AxisListType
ds = bass.ds

S = 1024
D = 1024
TILES = S // P
GRID_W = 64
HEAD = 64
N_GROUPS = 4
PER_GROUP = 8
N_EXPERTS = N_GROUPS * PER_GROUP
MOE_BLOCKS = -(-((2 * S + N_EXPERTS * (P - 1)) // P) // 2) * 2
ROW_BLOCKS = MOE_BLOCKS + 2
UNUSED_ROW = 4096
LN_EPS = 1e-5
RMS_EPS = 1e-6
NEG = -1e30
FULL_BIAS = 15 * GRID_W
INNER_BIAS = 9 * GRID_W


class Stage:

    def __init__(self, nc, name):
        self.nc, self.name = nc, name

    def __enter__(self):
        self.stack = ExitStack()
        self.sems = []
        self.marks = self.sem("marks")
        return self

    def sb(self, name, shape, dt=F32):
        return self.stack.enter_context(self.nc.sbuf_tensor(f"{self.name}_{name}", shape, dt))

    def ps(self, name, shape, dt=F32):
        return self.stack.enter_context(self.nc.psum_tensor(f"{self.name}_{name}", shape, dt))

    def sem(self, name):
        self.sems.append(self.nc.alloc_semaphore(f"{self.name}_{name}"))
        return self.sems[-1]

    def credit(self, pool, sems, source):
        spare = self.sb("spare", [1, 16])
        for sem in sems:
            pool.dma_start(spare[:, :], source[0:1, 0:16]).then_inc(sem, 16)
            pool.wait_ge(sem, 16)

    def block(self):
        return self.nc.Block()

    def __exit__(self, *error):
        if error[0] is None:
            self.nc.clear_and_free_semaphores(self.sems)
            self.nc.all_engine_barrier()
        return self.stack.__exit__(*error)


def held(eng, marks, sem, value):
    eng.wait_ge(sem, value)
    eng.sem_inc(marks, 1)


def rows(ap):
    return ap.rearrange("(t p) n -> p t n", p=P)


def modulation(nc, name, c, w, b, mod):
    KC, CW, RING = D // P, 512, 4
    N = w.shape[1]
    LOOPS = N // (CW * RING)
    wv = w.rearrange("(p c) n -> p c n", c=KC)
    with Stage(nc, name) as st:
        ccol = st.sb("ccol", [P, KC])
        cact = st.sb("cact", [P, KC])
        wt = st.sb("wt", [P, RING, KC, CW])
        brow = st.sb("brow", [1, N])
        out = st.sb("out", [1, N])
        acc = st.ps("acc", [P, RING, CW])
        c_in, b_in, stored = st.sem("c_in"), st.sem("b_in"), st.sem("stored")
        w_in = [st.sem(f"w_in{j}") for j in range(RING)]
        act_done, mm_done, added = st.sem("act_done"), st.sem("mm_done"), st.sem("added")
        with st.block() as block:

            @block.sync
            def _(sp):
                with sp.Fori(0, LOOPS) as i:
                    for j in range(RING):
                        sp.wait_ge(mm_done, i * RING + j + 1)
                        sp.dma_start(wt[:, j], wv[:, :, ds(i * (RING * CW) + j * CW, CW)]).then_inc(w_in[j], 16)
                sp.wait_ge(added, RING + RING * LOOPS)
                sp.dma_start(mod, out[:, :]).then_inc(stored, 16)
                sp.wait_ge(stored, 16)

            @block.scalar
            def _(act):
                act.dma_start(ccol[:, :], c.rearrange("a (p c) -> (a p) c", c=KC)).then_inc(c_in, 16)
                act.dma_start(brow[:, :], b).then_inc(b_in, 16)
                act.wait_ge(c_in, 16)
                act.activation(cact[:, :], ccol[:, :], ACT.Silu).then_inc(act_done, 1)

            @block.tensor
            def _(pe):
                pe.sem_inc(mm_done, RING)
                pe.wait_ge(act_done, 1)
                with pe.Fori(0, LOOPS) as i:
                    for j in range(RING):
                        pe.wait_ge(w_in[j], i * 16 + 16)
                        pe.wait_ge(added, i * RING + j + 1)
                        for k in range(KC):
                            last = pe.matmul(acc[0:1, j], cact[:, k:k + 1], wt[:, j, k], start=k == 0, stop=k == KC - 1)
                        last.then_inc(mm_done, 1)

            @block.vector
            def _(dve):
                dve.sem_inc(added, RING)
                dve.wait_ge(b_in, 16)
                with dve.Fori(0, LOOPS) as i:
                    for j in range(RING):
                        dve.wait_ge(mm_done, i * RING + RING + j + 1)
                        col = i * (RING * CW) + j * CW
                        dve.tensor_tensor(out[:, ds(col, CW)], acc[0:1, j], brow[:, ds(col, CW)],
                                          ALU.add).then_inc(added, 1)


def project(nc, name, src, w, dst, ident_dram):
    K, N = w.shape
    KC = K // P
    GROUPS = [(c, min(4, KC - c)) for c in range(0, KC, 4)]
    PAIRS = -(-N // 1024)
    CW = N // (2 * PAIRS)
    assert CW * 2 * PAIRS == N and len(GROUPS) <= 2
    wv = w.rearrange("(p c) n -> p c n", c=KC)
    src_tiles = src.rearrange("(t p) n -> t p n", p=P)
    dst_rows = rows(dst)
    with Stage(nc, name) as st:
        ident = st.sb("ident", [P, P])
        tok = st.sb("tok", [P, 2, K])
        srcT = st.sb("srcT", [P, KC, S])
        wt = st.sb("wt", [P, 2, KC, CW])
        out = st.sb("out", [P, 2, TILES, CW])
        tp = [st.ps(f"tp{e}", [P, 2, 512]) for e in range(2)]
        acc = [st.ps(f"acc{e}", [P, 2, 512]) for e in range(2)]
        id_in = st.sem("id_in")
        tok_in = [st.sem(f"tok_in{j}") for j in range(2)]
        w_in = [st.sem(f"w_in{j}") for j in range(2)]
        stored = [st.sem(f"stored{j}") for j in range(2)]
        turned, mm_done = st.sem("turned"), st.sem("mm_done")
        tok_used = st.sem("tok_used")
        copied = [st.sem(f"copied{e}") for e in range(2)]
        evac = [st.sem(f"evac{e}") for e in range(2)]
        with st.block() as block:

            @block.sync
            def _(sp):
                sp.dma_start(ident[:, :], ident_dram).then_inc(id_in, 16)
                with sp.Fori(0, TILES // 2) as i:
                    for j in range(2):
                        sp.wait_ge(tok_used, i * 2 + j + 1)
                        sp.dma_start(tok[:, j], src_tiles[ds(i * 2 + j, 1)].rearrange("a p n -> (a p) n")
                                     ).then_inc(tok_in[j], 16)
                with sp.Fori(0, PAIRS) as i:
                    for j in range(2):
                        sp.wait_ge(mm_done, (i * 2 + j) * TILES + TILES)
                        sp.dma_start(wt[:, j], wv[:, :, ds((i * 2 + j) * CW, CW)]).then_inc(w_in[j], 16)

            @block.tensor
            def _(pe):
                pe.sem_inc(tok_used, 2)
                pe.sem_inc(mm_done, 2 * TILES)
                pe.wait_ge(id_in, 16)
                with pe.Fori(0, TILES // 2) as i:
                    for j in range(2):
                        pe.wait_ge(tok_in[j], i * 16 + 16)
                        for e, (c0, nch) in enumerate(GROUPS):
                            pe.wait_ge(copied[e], i * 2 + j + 1)
                            for c in range(nch):
                                last = pe.transpose(tp[e][:, j, c * P:(c + 1) * P],
                                                    tok[:, j, c0 + c:K:KC], ident[:, :])
                            if e < len(GROUPS) - 1:
                                last.then_inc(turned, 1)
                        last.then_inc(tok_used, 1)
                for e in range(len(GROUPS)):
                    pe.wait_ge(copied[e], 2 + TILES)
                with pe.Fori(0, PAIRS) as i:
                    for j in range(2):
                        pe.wait_ge(w_in[j], i * 16 + 16)
                        for t in range(TILES):
                            e, m = t % 2, t // 2
                            pe.wait_ge(evac[e], (i * 2 + j) * (TILES // 2) + m + 1)
                            for k in range(KC):
                                last = pe.matmul(acc[e][:, m % 2, 0:CW], srcT[:, k, t * P:(t + 1) * P],
                                                 wt[:, j, k], start=k == 0, stop=k == KC - 1)
                            last.then_inc(mm_done, 1)

            def evacuate(eng, e, copy, store=None):
                eng.sem_inc(copied[e], 2)
                eng.sem_inc(evac[e], 2)
                if e < len(GROUPS):
                    c0, nch = GROUPS[e]
                    with eng.Fori(0, TILES // 2) as i:
                        for j in range(2):
                            if e < len(GROUPS) - 1:
                                eng.wait_ge(turned, i * 2 + j + 1)
                            else:
                                eng.wait_ge(tok_used, i * 2 + j + 3)
                            copy(srcT[:, c0:c0 + nch, ds((i * 2 + j) * P, P)],
                                 tp[e][:, j, 0:nch * P].rearrange("p (c s) -> p c s", c=nch)).then_inc(copied[e], 1)
                with eng.Fori(0, PAIRS) as i:
                    for j in range(2):
                        eng.wait_ge(stored[j], i * 16 + 1)
                        for m in range(TILES // 2):
                            t = 2 * m + e
                            eng.wait_ge(mm_done, (i * 2 + j) * TILES + t + 1 + 2 * TILES)
                            copy(out[:, j, t], acc[e][:, m % 2, 0:CW]).then_inc(evac[e], 1)
                        if store:
                            store(i, j)

            @block.vector
            def _(dve):
                evacuate(dve, 0, dve.tensor_copy)

            @block.scalar
            def _(act):
                for j in range(2):
                    act.sem_inc(stored[j], 1)

                def store(i, j):
                    for e in range(2):
                        held(act, st.marks, evac[e], (i * 2 + j + 1) * (TILES // 2) + 2)
                    act.dma_start(dst_rows[:, :, ds((i * 2 + j) * CW, CW)], out[:, j]).then_inc(stored[j], 16)

                evacuate(act, 1, lambda o, i: act.activation(o, i, ACT.Copy), store)
                for j in range(2):
                    act.wait_ge(stored[j], 16 * PAIRS + 1)


def neighbour_bias(nc, name, rpb, padded, bias, flip_dram):
    H, R, C = rpb.shape
    Q = GRID_W
    RING = 4
    SPLIT = 8
    with Stage(nc, name) as st:
        flat = st.sb("flat", [H, R * C])
        zero = st.sb("zero", [1, Q])
        flip = st.sb("flip", [Q, P])
        raw = st.sb("raw", [Q, H * R, Q])
        tab = st.sb("tab", [P, RING, FULL_BIAS + INNER_BIAS])
        turned = [st.ps(f"turned{n}", [P, 2, 512]) for n in range(2)]
        r_in, p_out, f_in, raw_in = (st.sem(n) for n in ("r_in", "p_out", "f_in", "raw_in"))
        stored = [st.sem(f"stored{j}") for j in range(RING)]
        zeroed, masked, flipped, copied, inner = (st.sem(n) for n in ("zeroed", "masked", "flipped", "copied", "inner"))
        with st.block() as block:

            @block.sync
            def _(sp):
                sp.dma_start(flat[:, :], rpb.rearrange("h r c -> h (r c)")).then_inc(r_in, 16)
                sp.dma_start(flip[:, :], flip_dram).then_inc(f_in, 16)
                sp.wait_ge(r_in, 16)
                sp.wait_ge(zeroed, 1)
                sp.dma_start(padded[0:1, R * C - Q:R * C], zero[:, :]).then_inc(p_out, 16)
                sp.dma_start(padded[1:H + 1, 0:R * C], flat[:, :]).then_inc(p_out, 16)
                sp.dma_start(padded[H + 1:H + 2, 0:Q], zero[:, :]).then_inc(p_out, 16)
                sp.wait_ge(p_out, 48)
                sp.dma_start(raw[:, :, :], bass.AP(tensor=padded.tensor, offset=R * C + C // 2 - (Q - 1),
                                                   ap=[[1, Q], [C, H * R], [1, Q]])).then_inc(raw_in, 16)

            @block.gpsimd
            def _(pool):
                pool.memset(zero[:, :], 0.0).then_inc(zeroed, 1)
                pool.wait_ge(raw_in, 16)
                left = raw[:, :, 0:48]
                pool.affine_select(out=left, in_=left, compare_op=ALU.is_ge, fill=NEG, base=8 - (Q - 1),
                                   pattern=[[0, H * R], [1, 48]], channel_multiplier=1).then_inc(masked, 1)
                pool.wait_ge(masked, 1)
                right = raw[:, :, 16:Q]
                pool.affine_select(out=right, in_=right, compare_op=ALU.is_gt, fill=NEG, base=8 - 16 + (Q - 1),
                                   pattern=[[0, H * R], [-1, 48]], channel_multiplier=-1).then_inc(masked, 1)
                for h in range(H):
                    r = h % RING
                    pool.wait_ge(copied, 5 * (h + 1))
                    pool.tensor_copy(tab[:, r, FULL_BIAS:], tab[:, r, 3 * Q:3 * Q + INNER_BIAS]).then_inc(inner, 1)
                    pool.wait_ge(inner, 3 * h + 1)
                    pool.memset(tab[0:64, r, FULL_BIAS + 8 * Q:], NEG).then_inc(inner, 1)
                    pool.memset(tab[64:P, r, FULL_BIAS:FULL_BIAS + Q], NEG).then_inc(inner, 1)
                    pool.wait_ge(inner, 3 * h + 3)
                    pool.dma_start(bias[h], tab[:, r]).then_inc(stored[r], 16)
                for r in range(RING):
                    pool.wait_ge(stored[r], 16 * (H // RING))

            @block.tensor
            def _(pe):
                pe.wait_ge(f_in, 16)
                pe.wait_ge(masked, 2)
                for h in range(H):
                    if h >= 2:
                        pe.wait_ge(copied, 5 * (h - 1))
                    for n, (a, b) in enumerate(((0, SPLIT), (SPLIT, R))):
                        last = pe.matmul(turned[h % 2][:, n, 0:(b - a) * Q], flip[:, :],
                                         raw[:, h * R + a:h * R + b, :].rearrange("q r k -> q (r k)"), start=True, stop=True)
                    last.then_inc(flipped, 1)

            @block.vector
            def _(dve):
                for h in range(H):
                    r = h % RING
                    if h >= RING:
                        dve.wait_ge(stored[r], 16 * (h // RING))
                    dve.wait_ge(flipped, h + 1)
                    ps = turned[h % 2]
                    dve.memset(tab[64:P, r, 0:Q], 0.0).then_inc(copied, 1)
                    dve.tensor_copy(tab[0:64, r, 0:SPLIT * Q], ps[0:64, 0, :]).then_inc(copied, 1)
                    dve.tensor_copy(tab[0:64, r, SPLIT * Q:R * Q], ps[0:64, 1, 0:(R - SPLIT) * Q]).then_inc(copied, 1)
                    dve.tensor_copy(tab[64:P, r, Q:(SPLIT + 1) * Q], ps[64:P, 0, :]).then_inc(copied, 1)
                    dve.tensor_copy(tab[64:P, r, (SPLIT + 1) * Q:R * Q], ps[64:P, 1, 0:(R - SPLIT - 1) * Q]).then_inc(copied, 1)


def neighbour_units():
    units = []
    for p in range(TILES):
        if p < 2:
            units.append((0, 512, (7 - 2 * p) * GRID_W))
        elif p < 6:
            units.append(((p - 2) * P, 9 * GRID_W, FULL_BIAS))
        else:
            units.append((512, 512, (15 - 2 * p) * GRID_W))
    return units


def attention(nc, name, q, k, v, o, ident_dram, *, groups, heads, shared, dk, scale, units, bias=None, diagonal=False, clear=None):
    dv = HEAD
    kv_heads = 1 if shared else heads
    U = heads * TILES
    q_scale = scale if bias is not None else 1.0
    exp_scale = 1.0 if bias is not None else scale

    counts = [0, 0]
    events = {}

    def event(key, e):
        events[key] = (e, counts[e])
        counts[e] += 1

    for a in range(kv_heads):
        for g in range(2):
            event(("k", a, g), g)
    for a in range(heads):
        for g in range(2):
            event(("q", a, g), g)
    qk_events = list(counts)
    key_groups = []
    for u in range(U):
        k0, nk, _ = units[u % TILES]
        tiles = [(i, min(P, nk - i * P)) for i in range(-(-nk // P))]
        key_groups.append([tiles[g:g + 4] for g in range(0, len(tiles), 4)])
        for g in range(len(key_groups[u])):
            event(("p", u, g), g)
    PER = list(counts)

    def cols(src, g, n, a, eng=None):
        ap, first, stride, width = src
        start = g * (n * stride) + (first + a * stride)
        return rows(ap)[:, :, ds(eng.snap(start) if eng else start, width)]

    with Stage(nc, name) as st:
        ident = st.sb("ident", [P, P])
        q_tok = st.sb("q_tok", [P, heads, TILES, dk])
        k_tok = st.sb("k_tok", [P, kv_heads, TILES, dk])
        v_tok = st.sb("v_tok", [P, kv_heads, TILES, dv])
        o_tok = st.sb("o_tok", [P, heads, TILES, dv])
        qT = st.sb("qT", [dk, heads, S])
        kT = st.sb("kT", [dk, kv_heads, S])
        probs = st.sb("probs", [P, 2, S])
        probsT = st.sb("probsT", [P, 2, TILES, P])
        stat = st.sb("stat", [P, 2, 4])
        if bias is not None:
            btab = st.sb("btab", [P, heads, FULL_BIAS + INNER_BIAS])
            biased = st.sb("biased", [P, 2, INNER_BIAS])
        scores = st.ps("scores", [P, 2, S])
        turn = [st.ps(f"turn{e}", [P, 512]) for e in range(2)]
        out = [st.ps(f"out{r}", [P, 512]) for r in range(2)]
        id_in, q_in, k_in, v_in, b_in = (st.sem(x) for x in ("id_in", "q_in", "k_in", "v_in", "b_in"))
        stored = st.sem("stored")
        s_ready, s_used, max_ready, p_ready = (st.sem(x) for x in ("s_ready", "s_used", "max_ready", "p_ready"))
        if bias is None:
            s_used = p_ready
        P0 = 2 if bias is None else 0
        small = st.sem("small")
        t_done = [st.sem(f"t_done{e}") for e in range(2)]
        evac = [st.sem(f"evac{e}") for e in range(2)]
        pv_done, o_done = st.sem("pv_done"), st.sem("o_done")
        SMALL = (1 if exp_scale != 1.0 else 0) + 1 + (1 if diagonal else 0)
        T0 = [PER[e] - qk_events[e] + 1 for e in range(2)]

        if clear is not None:
            zero = st.sb("zero", [P, D])
            zeroed, cleared = st.sem("zeroed"), st.sem("cleared")

        with st.block() as block:

            if clear is not None:
                @block.gpsimd
                def _(pool):
                    pool.memset(zero[:, :], 0.0).then_inc(zeroed, 1)
                    pool.wait_ge(zeroed, 1)
                    for n in range(clear.shape[0] // P):
                        pool.dma_start(clear[n * P:(n + 1) * P, :], zero[:, :]).then_inc(cleared, 16)
                        pool.wait_ge(cleared, 16 * (n + 1))

            @block.sync
            def _(sp):
                sp.dma_start(ident[:, :], ident_dram).then_inc(id_in, 16)
                with sp.Fori(0, groups) as g:
                    loads = [(k_tok[:, a], cols(k, g, kv_heads, a, sp)) for a in range(kv_heads)]
                    sp.wait_ge(t_done[1], g * PER[1] + 1)
                    for dst, part in loads:
                        sp.dma_start(dst, part).then_inc(k_in, 16)
                    for a in range(heads):
                        sp.dma_start(q_tok[:, a], cols(q, g, heads, a)).then_inc(q_in, 16)
                    sp.wait_ge(pv_done, g * U + 1)
                    for a in range(kv_heads):
                        sp.dma_start(v_tok[:, a], cols(v, g, kv_heads, a)).then_inc(v_in, 16)
                    if bias is not None:
                        sp.dma_start(btab[:, :, :], bias[ds(g * heads, heads)].rearrange("h p n -> p h n")
                                     ).then_inc(b_in, 16)

            @block.tensor
            def _(pe):
                pe.wait_ge(id_in, 16)
                for e in range(2):
                    pe.sem_inc(t_done[e], T0[e])
                pe.sem_inc(pv_done, 1)
                with pe.Fori(0, groups) as g:

                    def turns(key, sources, dest):
                        e, n = events[key]
                        pe.wait_ge(evac[e], g * PER[e] + n + 1)
                        if sources[0][1] < P:
                            pe.sem_inc(st.marks, 1)
                        for i, (src, size) in enumerate(sources):
                            last = pe.transpose(turn[e][0:size, i * P:(i + 1) * P], src, ident[:, :])
                        last.then_inc(t_done[e], 1)

                    pe.wait_ge(k_in, (g + 1) * (16 * kv_heads))
                    for a in range(kv_heads):
                        for h in range(2):
                            turns(("k", a, h), [(k_tok[:, a, 4 * h + i], dk) for i in range(4)], kT)
                    pe.wait_ge(q_in, (g + 1) * (16 * heads))
                    for a in range(heads):
                        for h in range(2):
                            turns(("q", a, h), [(q_tok[:, a, 4 * h + i], dk) for i in range(4)], qT)
                    for e in range(2):
                        pe.wait_ge(evac[e], g * PER[e] + qk_events[e] + 1)
                    pe.wait_ge(v_in, (g + 1) * (16 * kv_heads))

                    def score(u):
                        a, t, r = u // TILES, u % TILES, u % 2
                        kv = 0 if shared else a
                        k0, nk, _ = units[t]
                        pe.wait_ge(s_used, g * U + u + 1)
                        for c in range(0, nk, 512):
                            w = min(512, nk - c)
                            last = pe.matmul(scores[:, r, c:c + w], qT[:, a, t * P:(t + 1) * P],
                                             kT[:, kv, k0 + c:k0 + c + w], start=True, stop=True)
                        last.then_inc(s_ready, 1)

                    def turn_probs(u):
                        pe.wait_ge(p_ready, g * U + u + 1 + P0)
                        for n, tiles in enumerate(key_groups[u]):
                            turns(("p", u, n), [(probs[:, u % 2, i * P:i * P + size], size) for i, size in tiles], probsT)

                    def combine(u):
                        a, t, r = u // TILES, u % TILES, u % 2
                        kv = 0 if shared else a
                        k0 = units[t][0]
                        pe.wait_ge(o_done, g * U + u + 1)
                        flat = [x for tiles in key_groups[u] for x in tiles]
                        for n, (i, size) in enumerate(flat):
                            if i % 4 == 0:
                                e, m = events[("p", u, i // 4)]
                                pe.wait_ge(evac[e], g * PER[e] + m + 2)
                            last = pe.matmul(out[r][:, 0:dv], probsT[0:size, r, i],
                                             v_tok[0:size, kv, k0 // P + i], start=n == 0, stop=n == len(flat) - 1)
                        last.then_inc(pv_done, 1)

                    score(0)
                    score(1)
                    for u in range(U):
                        turn_probs(u)
                        if u + 2 < U:
                            score(u + 2)
                        combine(u)

            def evacuate(eng, e, g, key, dest, by=1.0):
                n = events[key][1]
                eng.wait_ge(t_done[e], g * PER[e] + n + 1 + T0[e])
                if e == 0:
                    ins = eng.tensor_scalar(dest[0], dest[1], by, None, ALU.mult)
                else:
                    ins = eng.activation(dest[0], dest[1], ACT.Copy, scale=by)
                ins.then_inc(evac[e], 1)

            def evacuate_qk(eng, e, g):
                for kind, n, dst, by in (("k", kv_heads, kT, 1.0), ("q", heads, qT, q_scale)):
                    for a in range(n):
                        evacuate(eng, e, g, (kind, a, e), (dst[:, a, e * 512:(e + 1) * 512], turn[e][0:dk, :]), by)

            def evacuate_p(eng, e, g, u):
                if e < len(key_groups[u]):
                    tiles = key_groups[u][e]
                    size = tiles[0][1]
                    n = len(tiles)
                    assert all(x[1] == size for x in tiles)
                    evacuate(eng, e, g, ("p", u, e),
                             (probsT[0:size, u % 2, 4 * e:4 * e + n], turn[e][0:size, 0:n * P].rearrange("p (n q) -> p n q", q=P)))

            @block.vector
            def _(dve):
                dve.sem_inc(evac[0], 1)
                dve.sem_inc(o_done, 2)
                if bias is not None:
                    dve.sem_inc(s_used, 2)
                with dve.Fori(0, groups) as g:
                    evacuate_qk(dve, 0, g)
                    if bias is not None:
                        dve.wait_ge(b_in, (g + 1) * 16)
                    n_small = 0

                    def done_small(ins):
                        nonlocal n_small
                        n_small += 1
                        ins.then_inc(small, 1)
                        dve.wait_ge(small, g * (U * SMALL) + n_small)


                    def row_max(u):
                        a, t, r = u // TILES, u % TILES, u % 2
                        k0, nk, b0 = units[t]
                        dve.wait_ge(s_ready, g * U + u + 1)
                        if bias is not None:
                            dve.tensor_tensor(biased[:, r, 0:nk], scores[:, r, 0:nk], btab[:, a, b0:b0 + nk],
                                              ALU.add).then_inc(s_used, 1)
                            dve.wait_ge(s_used, g * U + u + 3)
                            src = biased[:, r, 0:nk]
                        else:
                            src = scores[:, r, 0:nk]
                        if diagonal:
                            done_small(dve.memset(scores[0:64, r, nk - 64:nk], NEG))
                        if exp_scale != 1.0:
                            done_small(dve.tensor_reduce(stat[:, r, 0:1], src, AX.X, ALU.max, negate=True))
                            dve.tensor_scalar(stat[:, r, 1:2], stat[:, r, 0:1], exp_scale, None,
                                              ALU.mult).then_inc(max_ready, 1)
                        else:
                            dve.tensor_reduce(stat[:, r, 1:2], src, AX.X, ALU.max, negate=True).then_inc(max_ready, 1)

                    row_max(0)
                    row_max(1)
                    for u in range(U):
                        a, t, r = u // TILES, u % TILES, u % 2
                        dve.wait_ge(p_ready, g * U + u + 1 + P0)
                        done_small(dve.reciprocal(stat[:, r, 3:4], stat[:, r, 2:3]))
                        evacuate_p(dve, 0, g, u)
                        if u + 2 < U:
                            row_max(u + 2)
                        if u == 0:
                            dve.wait_ge(stored, g * (16 * heads) + 1)
                        dve.wait_ge(pv_done, g * U + u + 2)
                        dve.tensor_scalar(o_tok[:, a, t], out[r][:, 0:dv], stat[:, r, 3:4], None,
                                          ALU.mult).then_inc(o_done, 1)

            @block.scalar
            def _(act):
                act.sem_inc(evac[1], 1)
                act.sem_inc(stored, 1)
                if bias is None:
                    act.sem_inc(s_used, 2)
                with act.Fori(0, groups) as g:
                    evacuate_qk(act, 1, g)

                    def exponentials(u):
                        r = u % 2
                        nk = units[u % TILES][1]
                        src = biased[:, r, 0:nk] if bias is not None else scores[:, r, 0:nk]
                        act.wait_ge(max_ready, g * U + u + 1)
                        act.activation(probs[:, r, 0:nk], src, ACT.Exp, bias=stat[:, r, 1:2], scale=exp_scale,
                                       accum_out=stat[:, r, 2:3]).then_inc(p_ready, 1)

                    exponentials(0)
                    for u in range(U):
                        if u + 1 < U:
                            exponentials(u + 1)
                        evacuate_p(act, 1, g, u)
                    held(act, st.marks, o_done, (g + 1) * U + 2)
                    for a in range(heads):
                        act.dma_start(cols(o, g, heads, a), o_tok[:, a]).then_inc(stored, 16)
                act.wait_ge(stored, groups * 16 * heads + 1)


def steps(eng, sem, base):
    count = [0]

    def step(ins):
        count[0] += 1
        ins.then_inc(sem, 1)
        eng.wait_ge(sem, base + count[0])

    return step


def modulate(nc, name, x, mod, part, h):
    xv, hv = (v.rearrange("(t p) n -> t p n", p=P) for v in (x, h))
    with Stage(nc, name) as st:
        shift, scale, xt, ht = st.sb("shift", [P, D]), st.sb("scale", [P, D]), st.sb("xt", [P, 2, D]), st.sb("ht", [P, 2, D])
        m_in, ready, done = st.sem("m_in"), st.sem("ready"), st.sem("done")
        x_in, stored = [st.sem(f"x_in{j}") for j in range(2)], [st.sem(f"stored{j}") for j in range(2)]
        with st.block() as block:

            @block.sync
            def _(sp):
                for i, dst in enumerate((shift, scale)):
                    sp.dma_start(dst[:, :], mod[0, (part + i) * D:(part + i + 1) * D].partition_broadcast(P)).then_inc(m_in, 16)
                with sp.Fori(0, TILES // 2) as i:
                    for j in range(2):
                        sp.wait_ge(done, i * 4 + j * 2 + 2)
                        sp.dma_start(xt[:, j], xv[ds(i * 2 + j, 1)].rearrange("a p n -> (a p) n")).then_inc(x_in[j], 16)

            @block.vector
            def _(dve):
                dve.sem_inc(done, 4)
                dve.wait_ge(m_in, 32)
                dve.tensor_scalar(scale[:, :], scale[:, :], 1.0, None, ALU.add).then_inc(ready, 1)
                dve.wait_ge(ready, 1)
                with dve.Fori(0, TILES // 2) as i:
                    step = steps(dve, done, i * 4 + 4)
                    for j in range(2):
                        dve.wait_ge(x_in[j], i * 16 + 16)
                        dve.wait_ge(stored[j], i * 16 + 1)
                        step(dve.tensor_tensor(ht[:, j], xt[:, j], scale[:, :], ALU.mult))
                        step(dve.tensor_tensor(ht[:, j], ht[:, j], shift[:, :], ALU.add))

            @block.scalar
            def _(act):
                for j in range(2):
                    act.sem_inc(stored[j], 1)
                with act.Fori(0, TILES // 2) as i:
                    for j in range(2):
                        act.wait_ge(done, i * 4 + j * 2 + 6)
                        act.dma_start(hv[ds(i * 2 + j, 1)].rearrange("a p n -> (a p) n"), ht[:, j]).then_inc(stored[j], 16)
                for j in range(2):
                    act.wait_ge(stored[j], 16 * TILES // 2 + 1)


def residual_norm(nc, name, x, mod, part, ln_g, ln_b, alpha, x_out, *, y=None, experts=None, nxt=None):
    tile = lambda v: v.rearrange("(t p) n -> t p n", p=P)
    at = lambda v, n: tile(v)[ds(n, 1)].rearrange("a p n -> (a p) n")
    HALF = D // 2
    VS = 9 if experts else 7
    V = 2 * VS + 2 + 4
    PL = 2
    with Stage(nc, name) as st:
        gate, g, b = (st.sb(n, [P, D]) for n in ("gate", "g", "b"))
        xt, yt, z, xn = (st.sb(n, [P, 2, D]) for n in ("xt", "yt", "z", "xn"))
        bn, mv, inv, rstd, shift0 = st.sb("bn", [P, 2, 2, 6]), st.sb("mv", [P, 2, 2]), st.sb("inv", [P, 2]), st.sb("rstd", [P, 2]), st.sb("shift0", [P, 2])
        consts = [(gate, mod[0, part * D:(part + 1) * D]), (g, ln_g), (b, ln_b)]
        if nxt:
            shift, scale, h = st.sb("shift", [P, D]), st.sb("scale", [P, D]), st.sb("h", [P, 2, D])
            consts += [(shift, nxt[0][0, nxt[1] * D:(nxt[1] + 1) * D]), (scale, nxt[0][0, (nxt[1] + 1) * D:(nxt[1] + 2) * D])]
        if experts:
            y2t = st.sb("y2t", [P, 2, D])
            places, gates, idx = st.sb("places", [P, 2, TILES + 2], U32), st.sb("gates", [P, 2, TILES]), st.sb("idx", [P, 2, 2], U32)
            e_in, picked = st.sem("e_in"), st.sem("picked")
        c_in, ready = st.sem("c_in"), st.sem("ready")
        x_in, y_in, x_st, h_st = ([st.sem(f"{n}{j}") for j in range(2)] for n in ("x_in", "y_in", "x_st", "h_st"))
        dv, ac, pl = st.sem("dv"), st.sem("ac"), st.sem("pl")
        with st.block() as block:

            @block.sync
            def _(sp):
                for dst, src in consts:
                    sp.dma_start(dst[:, :], src.partition_broadcast(P)).then_inc(c_in, 16)
                if experts:
                    sp.dma_start(places[:, :, 0:TILES], experts[1]).then_inc(e_in, 16)
                    sp.dma_start(gates[:, :, :], experts[2]).then_inc(e_in, 16)
                with sp.Fori(0, TILES // 2) as i:
                    for j in range(2):
                        sp.wait_ge(dv, i * V + j * VS + VS - 5)
                        sp.dma_start(xt[:, j], at(x, i * 2 + j)).then_inc(x_in[j], 16)
                        if y is not None:
                            sp.dma_start(yt[:, j], at(y, i * 2 + j)).then_inc(y_in[j], 16)

            @block.vector
            def _(dve):
                dve.sem_inc(dv, V)
                dve.wait_ge(c_in, 16 * len(consts))
                dve.tensor_scalar(gate[:, :], gate[:, :], 1.0, None, ALU.add).then_inc(ready, 1)
                if nxt:
                    dve.tensor_scalar(scale[:, :], scale[:, :], 1.0, None, ALU.add).then_inc(ready, 1)
                    dve.wait_ge(ready, 2)
                if experts:
                    dve.wait_ge(e_in, 32)
                dve.wait_ge(ready, 1)
                with dve.Fori(0, TILES // 2) as i:
                    step = steps(dve, dv, i * V + V)
                    for j in range(2):
                        dve.wait_ge(ac, i * 4 + 3 + j)
                        dve.wait_ge(x_in[j], i * 16 + 16)
                        if experts:
                            dve.wait_ge(y_in[j], i * 32 + 32)
                            g1, g2 = (gates[:, n, ds(i * 2 + j, 1)] for n in range(2))
                            step(dve.tensor_scalar(z[:, j], yt[:, j], g1, None, ALU.mult))
                            step(dve.scalar_tensor_tensor(z[:, j], y2t[:, j], g2, z[:, j], ALU.mult, ALU.add))
                            step(dve.tensor_tensor(z[:, j], z[:, j], gate[:, :], ALU.mult))
                        else:
                            dve.wait_ge(y_in[j], i * 16 + 16)
                            step(dve.tensor_tensor(z[:, j], yt[:, j], gate[:, :], ALU.mult))
                        step(dve.scalar_tensor_tensor(z[:, j], xt[:, j], alpha, z[:, j], ALU.mult, ALU.add))
                        step(dve.bn_stats(bn[:, j, 0], z[:, j, 0:HALF]))
                        step(dve.bn_stats(bn[:, j, 1], z[:, j, HALF:]))
                        dve.sem_inc(st.marks, 1)
                        step(dve.bn_aggr(mv[:, j], bn[:, j]))
                        step(dve.tensor_scalar(inv[:, j:j + 1], mv[:, j, 1:2], LN_EPS, None, ALU.add))
                        step(dve.reciprocal(inv[:, j:j + 1], inv[:, j:j + 1]))
                    for j in range(2):
                        dve.wait_ge(ac, i * 4 + 4 + j + 1)
                        step(dve.scalar_tensor_tensor(shift0[:, j:j + 1], mv[:, j, 0:1], -1.0, rstd[:, j:j + 1], ALU.mult, ALU.mult))
                    for j in range(2):
                        dve.wait_ge(ac, i * 4 + 4 + 3 + j)
                        step(dve.tensor_tensor(xn[:, j], xn[:, j], g[:, :], ALU.mult))
                        step(dve.tensor_tensor(xn[:, j], xn[:, j], b[:, :], ALU.add))

            @block.scalar
            def _(act):
                act.sem_inc(ac, 4)
                with act.Fori(0, TILES // 2) as i:
                    for j in range(2):
                        act.wait_ge(dv, i * V + V + (j + 1) * VS)
                        act.activation(rstd[:, j:j + 1], inv[:, j:j + 1], ACT.Sqrt).then_inc(ac, 1)
                    for j in range(2):
                        act.wait_ge(dv, i * V + V + 2 * VS + j + 1)
                        if nxt:
                            act.wait_ge(pl, i * (2 * PL) + j * PL + 1)
                        act.wait_ge(x_st[j], i * 16 + 16)
                        act.activation(xn[:, j], z[:, j], ACT.Identity, scale=rstd[:, j:j + 1],
                                       bias=shift0[:, j:j + 1]).then_inc(ac, 1)

            @block.gpsimd
            def _(pool):
                pool.sem_inc(pl, 2 * PL)
                st.credit(pool, x_st + h_st, mod)
                if experts:
                    pool.wait_ge(e_in, 32)

                def gather(i, j):
                    for k in range(2):
                        pool.tensor_copy(idx[:, j, k:k + 1], places[:, k, ds(i * 2 + j, 1)]).then_inc(picked, 1)
                    held(pool, st.marks, picked, i * 4 + j * 2 + 2)
                    for k, dst in enumerate((yt, y2t)):
                        pool.indirect_dma_start(out=dst[:, j], out_offset=None, in_=experts[0],
                                                in_offset=bass.IndirectOffsetOnAxis(ap=idx[:, j, k:k + 1], axis=0)
                                                ).then_inc(y_in[j], 16)

                if experts:
                    for j in range(2):
                        gather(0, j)
                if nxt:
                    pool.wait_ge(ready, 2)
                with pool.Fori(0, TILES // 2) as i:
                    if experts:
                        with pool.If(i < TILES // 2 - 1):
                            for j in range(2):
                                pool.wait_ge(dv, i * V + V + j * VS + VS - 5)
                                gather(i + 1, j)
                    step = steps(pool, pl, i * (2 * PL) + 2 * PL)
                    for j in range(2):
                        pool.wait_ge(dv, i * V + V + 2 * VS + 2 + 2 * (j + 1))
                        pool.sem_inc(st.marks, 1)
                        pool.dma_start(at(x_out, i * 2 + j), xn[:, j]).then_inc(x_st[j], 16)
                        if nxt:
                            pool.wait_ge(h_st[j], i * 16 + 16)
                            step(pool.tensor_tensor(h[:, j], xn[:, j], scale[:, :], ALU.mult))
                            step(pool.tensor_tensor(h[:, j], h[:, j], shift[:, :], ALU.add))
                            pool.sem_inc(st.marks, 1)
                            pool.dma_start(at(nxt[2], i * 2 + j), h[:, j]).then_inc(h_st[j], 16)
                for j in range(2):
                    pool.wait_ge(x_st[j], 16 * TILES // 2 + 16)
                    if nxt:
                        pool.wait_ge(h_st[j], 16 * TILES // 2 + 16)


def route(nc, name, logits, bias, a, layer, row_table, plan, places, gates):
    G, E, T = N_GROUPS, PER_GROUP, TILES
    with Stage(nc, name) as st:
        sb = st.sb
        raw, lg, bt, cst = sb("raw", [P, T, G + N_EXPERTS]), sb("lg", [P, T, G + N_EXPERTS]), sb("bt", [P, G + N_EXPERTS]), sb("cst", [P, a["moe_const"].shape[1]])
        tri, ones = sb("tri", [P, P]), sb("ones", [P, P])
        tok_id = sb("tok_id", [P, T], U32)
        m, gs, ge, gsum, gprob = sb("m", [P, T]), sb("gs", [P, T, G]), sb("ge", [P, T, G]), sb("gsum", [P, T]), sb("gprob", [P, T])
        gfirst, og = sb("gfirst", [P, T, G]), sb("og", [P, T, G])
        sel, le, le2 = sb("sel", [P, T, G, E]), sb("le", [P, T, E]), sb("le2", [P, T, E])
        first, top = sb("first", [P, T, E]), [sb(f"top{k}", [P, T]) for k in range(2)]
        hot = [sb(f"hot{k}", [P, T, E]) for k in range(2)]
        diff, ediff, den, gt = sb("diff", [P, T]), sb("ediff", [P, T]), sb("den", [P, T]), sb("gt", [P, 2, T])
        oh = [sb(f"oh{k}", [P, T, G, E]) for k in range(2)]
        both = sb("both", [P, T, N_EXPERTS])
        cnt, over, nb, cum, start = sb("cnt", [P, N_EXPERTS]), sb("over", [P, N_EXPERTS, T]), sb("nb", [P, N_EXPERTS]), sb("cum", [P, N_EXPERTS]), sb("start", [P, N_EXPERTS])
        place, prod, pf, pu = sb("place", [P, T, N_EXPERTS]), sb("prod", [P, T, N_EXPERTS]), sb("pf", [P, 2, T]), sb("pu", [P, 2, T], U32)
        below, be = sb("below", [P, MOE_BLOCKS, N_EXPERTS]), sb("be", [P, MOE_BLOCKS])
        used, pf_plan, plan_t = sb("used", [P, MOE_BLOCKS // 2]), sb("pf_plan", [P, MOE_BLOCKS + 1]), sb("plan_t", [P, MOE_BLOCKS + 1], U32)
        empty = sb("empty", [P, ROW_BLOCKS], U32)
        rank, total = st.ps("rank", [P, T, N_EXPERTS]), st.ps("total", [P, 512])
        l_in, d, e_done, pe_done, filled, t_st, out_st, e_set = (
            st.sem(n) for n in ("l_in", "d", "e_done", "pe_done", "filled", "t_st", "out_st", "e_set"))
        rank_g, rank_e = cst[:, 0:G], cst[:, G:G + E]
        thr, blk = cst[:, 12:12 + T], cst[:, 20:20 + MOE_BLOCKS]
        over_t = lambda v: v.unsqueeze(1).to_broadcast([P, T, v.shape[1]])
        col = lambda v, n: v.unsqueeze(2).to_broadcast([P, T, n])
        at = {}
        with st.block() as block:

            @block.vector
            def _(dve):
                step_ = steps(dve, d, 0)
                n = [0]

                def step(ins, tag=None):
                    step_(ins)
                    n[0] += 1
                    if tag:
                        at[tag] = n[0]

                dve.wait_ge(l_in, 16 * 6)
                step(dve.tensor_tensor(lg[:, :, :], raw[:, :, :], over_t(bt[:, :]), ALU.add))
                step(dve.tensor_reduce(m[:, :], lg[:, :, 0:G], AX.X, ALU.max))
                step(dve.tensor_tensor(gs[:, :, :], lg[:, :, 0:G], col(m[:, :], G), ALU.subtract), "gs")
                step(dve.tensor_scalar(gfirst[:, :, :], gs[:, :, :], 0.0, None, ALU.is_equal))
                step(dve.tensor_tensor(gfirst[:, :, :], gfirst[:, :, :], over_t(rank_g), ALU.mult))
                step(dve.tensor_reduce(m[:, :], gfirst[:, :, :], AX.X, ALU.max))
                step(dve.tensor_tensor(og[:, :, :], gfirst[:, :, :], col(m[:, :], G), ALU.is_equal))
                for t in range(T):
                    step(dve.tensor_tensor(sel[:, t], lg[:, t, G:].rearrange("p (g e) -> p g e", g=G),
                                           og[:, t].unsqueeze(2).to_broadcast([P, G, E]), ALU.mult))
                step(dve.tensor_reduce(le[:, :, :], sel[:, :, :, :].rearrange("p t g e -> p t e g"), AX.X, ALU.add))
                for k, src in enumerate((le, le2)):
                    if k:
                        step(dve.scalar_tensor_tensor(le2[:, :, :], hot[0][:, :, :], NEG, le[:, :, :], ALU.mult, ALU.add))
                    step(dve.tensor_reduce(top[k][:, :], src[:, :, :], AX.X, ALU.max))
                    step(dve.tensor_tensor(first[:, :, :], src[:, :, :], col(top[k][:, :], E), ALU.is_equal))
                    step(dve.tensor_tensor(first[:, :, :], first[:, :, :], over_t(rank_e), ALU.mult))
                    step(dve.tensor_reduce(m[:, :], first[:, :, :], AX.X, ALU.max))
                    step(dve.tensor_tensor(hot[k][:, :, :], first[:, :, :], col(m[:, :], E), ALU.is_equal))
                step(dve.tensor_tensor(diff[:, :], top[1][:, :], top[0][:, :], ALU.subtract), "diff")
                for k in range(2):
                    for t in range(T):
                        step(dve.tensor_tensor(oh[k][:, t], og[:, t].unsqueeze(2).to_broadcast([P, G, E]),
                                               hot[k][:, t].unsqueeze(1).to_broadcast([P, G, E]), ALU.mult))
                flat = [o[:, :, :, :].rearrange("p t g e -> p t (g e)") for o in oh]
                step(dve.tensor_tensor(both[:, :, :], flat[0], flat[1], ALU.add), "both")
                dve.wait_ge(e_done, 2)
                step(dve.tensor_reduce(gsum[:, :], ge[:, :, :], AX.X, ALU.add))
                step(dve.reciprocal(gprob[:, :], gsum[:, :]))
                step(dve.tensor_scalar(den[:, :], ediff[:, :], 1.0, None, ALU.add))
                step(dve.reciprocal(den[:, :], den[:, :]))
                step(dve.tensor_tensor(gt[:, 0], den[:, :], gprob[:, :], ALU.mult))
                step(dve.tensor_tensor(gt[:, 1], gt[:, 0], ediff[:, :], ALU.mult), "gates")
                dve.wait_ge(pe_done, 1)
                step(dve.tensor_copy(cnt[:, :], total[:, 0:N_EXPERTS]))
                step(dve.tensor_tensor(over[:, :, :], cnt[:, :].unsqueeze(2).to_broadcast([P, N_EXPERTS, T]),
                                       thr.unsqueeze(1).to_broadcast([P, N_EXPERTS, T]), ALU.is_gt))
                step(dve.tensor_reduce(nb[:, :], over[:, :, :], AX.X, ALU.add))
                step(dve.tensor_tensor_scan(cum[:, :], ones[:, 0:N_EXPERTS], nb[:, :], 0.0, ALU.mult, ALU.add))
                step(dve.tensor_tensor(start[:, :], cum[:, :], nb[:, :], ALU.subtract))
                step(dve.tensor_scalar(start[:, :], start[:, :], float(P), None, ALU.mult))
                step(dve.tensor_tensor(place[:, :, :], rank[:, :, :], over_t(start[:, :]), ALU.add))
                for k in range(2):
                    step(dve.tensor_tensor(prod[:, :, :], place[:, :, :], flat[k], ALU.mult))
                    step(dve.tensor_reduce(pf[:, k], prod[:, :, :], AX.X, ALU.add))
                step(dve.tensor_copy(pu[:, :, :], pf[:, :, :]), "places")
                step(dve.tensor_tensor(below[:, :, :], blk.unsqueeze(2).to_broadcast([P, MOE_BLOCKS, N_EXPERTS]),
                                       cum[:, :].unsqueeze(1).to_broadcast([P, MOE_BLOCKS, N_EXPERTS]), ALU.is_ge))
                step(dve.tensor_reduce(be[:, :], below[:, :, :], AX.X, ALU.add))
                step(dve.tensor_scalar(pf_plan[:, 1:], be[:, :], float(N_EXPERTS - 1), float(layer * N_EXPERTS), ALU.min, ALU.add))
                step(dve.tensor_tensor(used[:, :], blk[:, ::2], cum[:, N_EXPERTS - 1:].to_broadcast([P, MOE_BLOCKS // 2]), ALU.is_lt))
                step(dve.tensor_reduce(pf_plan[:, 0:1], used[:, :], AX.X, ALU.add))
                step(dve.tensor_copy(plan_t[:, :], pf_plan[:, :]), "plan")

            @block.scalar
            def _(act):
                act.wait_ge(d, at["gs"])
                act.activation(ge[:, :, :], gs[:, :, :], ACT.Exp).then_inc(e_done, 1)
                act.wait_ge(d, at["diff"])
                act.activation(ediff[:, :], diff[:, :], ACT.Exp).then_inc(e_done, 1)

            @block.tensor
            def _(pe):
                pe.wait_ge(d, at["both"])
                for t in range(T):
                    pe.matmul(total[:, 0:N_EXPERTS], ones[:, :], both[:, t], start=t == 0, stop=t == T - 1)
                for t in range(T):
                    for s in range(t):
                        pe.matmul(rank[:, t], ones[:, :], both[:, s], start=s == 0, stop=False)
                    last = pe.matmul(rank[:, t], tri[:, :], both[:, t], start=t == 0, stop=True)
                last.then_inc(pe_done, 1)

            @block.sync
            def _(sp):
                for dst, src in ((raw[:, :, :], rows(logits)), (bt[:, :], bias.partition_broadcast(P)), (cst[:, :], a["moe_const"]),
                                 (tri[:, :], a["tri"]), (ones[:, :], a["ones"]), (tok_id[:, :], a["tok_id"])):
                    sp.dma_start(dst, src).then_inc(l_in, 16)
                sp.wait_ge(e_set, 1)
                sp.dma_start(row_table.rearrange("(p b) o -> p (b o)", p=P), empty[:, :]).then_inc(filled, 16)
                sp.wait_ge(d, at["gates"])
                sp.dma_start(gates, gt[:, :, :]).then_inc(out_st, 16)
                sp.wait_ge(d, at["places"])
                sp.dma_start(places, pu[:, :, :]).then_inc(out_st, 16)
                sp.wait_ge(d, at["plan"])
                sp.dma_start(plan, plan_t[0:1, :]).then_inc(out_st, 16)
                sp.wait_ge(out_st, 48)

            @block.gpsimd
            def _(pool):
                pool.memset(empty[:, :], UNUSED_ROW).then_inc(e_set, 1)
                pool.wait_ge(filled, 16)
                pool.wait_ge(l_in, 16 * 6)
                pool.wait_ge(d, at["places"])
                for k in range(2):
                    for t in range(T):
                        pool.indirect_dma_start(out=row_table, out_offset=bass.IndirectOffsetOnAxis(ap=pu[:, k, t:t + 1], axis=0),
                                                in_=tok_id[:, t:t + 1], in_offset=None).then_inc(t_st, 16)
                pool.wait_ge(t_st, 16 * 2 * T)


def experts(nc, name, h, row_table, plan, wg, wu, wd, y, ident_dram):
    F = wg.shape[-1]
    KC, FC = D // P, F // P
    by_expert = lambda w: w.rearrange("l e (p c) f -> (l e) p (c f)", p=P)
    wge, wue, wde = by_expert(wg), by_expert(wu), by_expert(wd)
    LAYERS_EXPERTS = wg.shape[0] * N_EXPERTS
    LOOPS = MOE_BLOCKS // 2
    with Stage(nc, name) as st:
        ident = st.sb("ident", [P, P])
        pl, ri = st.sb("pl", [1, MOE_BLOCKS + 1], U32), st.sb("ri", [P, ROW_BLOCKS], U32)
        rcol = st.sb("rcol", [P, 2], U32)
        x, xT = st.sb("x", [P, 2, D]), st.sb("xT", [P, 2, KC, P])
        g, u = st.sb("g", [P, 2, KC * F]), st.sb("u", [P, 2, KC * F])
        dn = st.sb("dn", [P, 2, FC * D])
        sg, hid, hidT, yt = st.sb("sg", [P, F]), st.sb("hid", [P, F]), st.sb("hidT", [P, FC, P]), st.sb("yt", [P, 2, D])
        xp = [st.ps(f"xp{e}", [P, 512]) for e in range(2)]
        gp, up, hp = st.ps("gp", [P, 512]), st.ps("up", [P, 512]), st.ps("hp", [P, 512])
        yp = [st.ps(f"yp{e}", [P, 512]) for e in range(2)]
        i_in, zeroed, picked = st.sem("i_in"), st.sem("zeroed"), st.sem("picked")
        x_in, gu_in, dn_in, stored = ([st.sem(f"{n}{j}") for j in range(2)] for n in ("x_in", "gu_in", "dn_in", "stored"))
        xt_done, gu_done, ht_done, dn_done = (st.sem(n) for n in ("xt_done", "gu_done", "ht_done", "dn_done"))
        x_cp = [st.sem(f"x_cp{e}") for e in range(2)]
        y_cp = [st.sem(f"y_cp{e}") for e in range(2)]
        sg_done, hid_done, ht_cp = (st.sem(n) for n in ("sg_done", "hid_done", "ht_cp"))
        half = [slice(0, 4), slice(4, 8)]

        def pairs_used(eng):
            eng.wait_ge(i_in, 48)
            return eng.value_load(pl[0:1, 0:1], min_val=1, max_val=LOOPS)

        with st.block() as block:

            @block.sync
            def _(sp):
                sp.dma_start(ident[:, :], ident_dram).then_inc(i_in, 16)
                sp.dma_start(pl[:, :], plan).then_inc(i_in, 16)
                with nc.allow_non_contiguous_dma(reason="one token number per row"):
                    sp.dma_start(ri[:, :], row_table.rearrange("(b p) o -> p (b o)", p=P)).then_inc(i_in, 16)
                pairs = pairs_used(sp)
                with sp.Fori(0, LOOPS) as i:
                    with sp.If(i < pairs):
                        for j in range(2):
                            expert = sp.value_load(pl[0:1, ds(i * 2 + j + 1, 1)], min_val=0, max_val=LAYERS_EXPERTS - 1)
                            sp.wait_ge(gu_done, i * 2 + j + 1)
                            for dst, src in ((g, wge), (u, wue)):
                                sp.dma_start(dst[:, j], src[ds(expert, 1)].rearrange("a p n -> (a p) n")).then_inc(gu_in[j], 16)
                            sp.wait_ge(dn_done, i * 2 + j + 1)
                            sp.dma_start(dn[:, j], wde[ds(expert, 1)].rearrange("a p n -> (a p) n")).then_inc(dn_in[j], 16)
                for j in range(2):
                    held(sp, st.marks, stored[j], pairs * 16 + 1)

            @block.gpsimd
            def _(pool):
                pool.memset(x[:, :, :], 0.0).then_inc(zeroed, 1)
                pool.wait_ge(i_in, 48)
                pool.wait_ge(zeroed, 1)

                def gather_x(j, column, count):
                    pool.tensor_copy(rcol[:, j:j + 1], column).then_inc(picked, 1)
                    held(pool, st.marks, picked, count)
                    pool.indirect_dma_start(out=x[:, j], out_offset=None, in_=h,
                                            in_offset=bass.IndirectOffsetOnAxis(ap=rcol[:, j:j + 1], axis=0),
                                            bounds_check=S - 1, oob_is_err=False).then_inc(x_in[j], 16)

                pairs = pairs_used(pool)
                gather_x(0, ri[:, 0:1], 1)
                with pool.Fori(0, LOOPS) as i:
                    with pool.If(i < pairs):
                        for j in range(2):
                            pool.wait_ge(xt_done, i * 2 + j + 1)
                            gather_x(1 - j, ri[:, ds(i * 2 + j + 1, 1)], i * 2 + j + 2)

            @block.tensor
            def _(pe):
                pe.sem_inc(gu_done, 2)
                pe.sem_inc(xt_done, 1)
                pe.sem_inc(dn_done, 2)
                pairs = pairs_used(pe)

                def turn_x(j):
                    for e in range(2):
                        for c in range(4):
                            last = pe.transpose(xp[e][:, c * P:(c + 1) * P], x[:, j, 4 * e + c:D:KC], ident[:, :])
                    last.then_inc(xt_done, 1)

                pe.wait_ge(x_in[0], 16)
                turn_x(0)
                with pe.Fori(0, LOOPS) as i:
                    with pe.If(i < pairs):
                        for j in range(2):
                            n = i * 2 + j
                            pe.wait_ge(gu_in[j], i * 32 + 32)
                            for e in range(2):
                                pe.wait_ge(x_cp[e], n + 1)
                            pe.wait_ge(hid_done, n + 1)
                            for k in range(KC):
                                pe.matmul(gp[:, 0:F], xT[:, j, k], g[:, j, k * F:(k + 1) * F], start=k == 0, stop=k == KC - 1)
                                last = pe.matmul(up[:, 0:F], xT[:, j, k], u[:, j, k * F:(k + 1) * F], start=k == 0, stop=k == KC - 1)
                            last.then_inc(gu_done, 1)
                            pe.wait_ge(x_in[1 - j], i * 16 + 16 * (j + 1))
                            turn_x(1 - j)
                            pe.wait_ge(hid_done, n + 2)
                            for c in range(FC):
                                last = pe.transpose(hp[:, c * P:(c + 1) * P], hid[:, c:F:FC], ident[:, :])
                            last.then_inc(ht_done, 1)
                            pe.wait_ge(dn_in[j], i * 16 + 16)
                            for e in range(2):
                                pe.wait_ge(y_cp[e], n + 1)
                            pe.wait_ge(ht_cp, n + 1)
                            for k in range(FC):
                                for e in range(2):
                                    last = pe.matmul(yp[e][:, :], hidT[:, k], dn[:, j, k * D + e * 512:k * D + (e + 1) * 512],
                                                     start=k == 0, stop=k == FC - 1)
                            last.then_inc(dn_done, 1)

            def copy_x(eng, copy, e, j, count):
                eng.wait_ge(xt_done, count)
                copy(xT[:, j, half[e]], xp[e][:, :].rearrange("p (c s) -> p c s", c=4)).then_inc(x_cp[e], 1)

            def copy_y(eng, copy, e, i, j):
                eng.wait_ge(stored[j], i * 16 + 1)
                eng.wait_ge(dn_done, i * 2 + j + 3)
                copy(yt[:, j, e * 512:(e + 1) * 512], yp[e][:, :]).then_inc(y_cp[e], 1)

            @block.scalar
            def _(act):
                act_copy = lambda o, i_: act.activation(o, i_, ACT.Copy)
                act.sem_inc(y_cp[1], 1)
                for j in range(2):
                    act.sem_inc(stored[j], 1)
                pairs = pairs_used(act)
                copy_x(act, act_copy, 1, 0, 2)
                with act.Fori(0, LOOPS) as i:
                    with act.If(i < pairs):
                        for j in range(2):
                            n = i * 2 + j
                            act.wait_ge(gu_done, n + 3)
                            act.activation(sg[:, :], gp[:, 0:F], ACT.Silu).then_inc(sg_done, 1)
                            copy_x(act, act_copy, 1, 1 - j, n + 3)
                            act.wait_ge(ht_done, n + 1)
                            act_copy(hidT[:, :, :], hp[:, 0:FC * P].rearrange("p (c s) -> p c s", c=FC)).then_inc(ht_cp, 1)
                            copy_y(act, act_copy, 1, i, j)
                            for e in range(2):
                                act.wait_ge(y_cp[e], n + 2)
                            act.dma_start(y[ds(i * (2 * P) + j * P, P), :], yt[:, j]).then_inc(stored[j], 16)

            @block.vector
            def _(dve):
                dve.sem_inc(y_cp[0], 1)
                dve.sem_inc(hid_done, 1)
                pairs = pairs_used(dve)
                copy_x(dve, dve.tensor_copy, 0, 0, 2)
                with dve.Fori(0, LOOPS) as i:
                    with dve.If(i < pairs):
                        for j in range(2):
                            n = i * 2 + j
                            dve.wait_ge(sg_done, n + 1)
                            dve.tensor_tensor(hid[:, :], sg[:, :], up[:, 0:F], ALU.mult).then_inc(hid_done, 1)
                            copy_x(dve, dve.tensor_copy, 0, 1 - j, n + 3)
                            copy_y(dve, dve.tensor_copy, 0, i, j)


def tile_at(v, n):
    return v.rearrange("(t p) n -> t p n", p=P)[ds(n, 1)].rearrange("a p n -> (a p) n")


def row_stage(nc, st, loads, consts, stores, vector_steps, body, acts):
    V, A = vector_steps, len(acts)
    c_in, dv, ac = st.sem("c_in"), st.sem("dv"), st.sem("ac")
    x_in, stored = [st.sem(f"x_in{j}") for j in range(2)], [st.sem(f"stored{j}") for j in range(2)]
    with st.block() as block:

        @block.sync
        def _(sp):
            for dst, src in consts:
                sp.dma_start(dst, src).then_inc(c_in, 16)
            with sp.Fori(0, TILES // 2) as i:
                for j in range(2):
                    n = i * 2 + j
                    held(sp, st.marks, dv, n * V + V)
                    for dst, src in loads:
                        sp.dma_start(dst(j), src(n)).then_inc(x_in[j], 16)

        @block.scalar
        def _(act):
            with act.Fori(0, TILES // 2) as i:
                for j in range(2):
                    n = i * 2 + j
                    act.wait_ge(x_in[j], i * (16 * len(loads)) + 16 * len(loads))
                    for m, (count, run) in enumerate(acts):
                        if m:
                            act.wait_ge(ac, n * A + m)
                        if count:
                            act.wait_ge(dv, n * V + 2 * V + count)
                        run(act, j).then_inc(ac, 1)

        @block.vector
        def _(dve):
            dve.sem_inc(dv, 2 * V)
            if consts:
                dve.wait_ge(c_in, 16 * len(consts))
            with dve.Fori(0, TILES // 2) as i:
                for j in range(2):
                    n = i * 2 + j
                    dve.wait_ge(x_in[j], i * (16 * len(loads)) + 16 * len(loads))
                    dve.wait_ge(stored[j], i * (16 * len(stores)) + 16)
                    body(dve, steps(dve, dv, n * V + 2 * V), j, lambda m: dve.wait_ge(ac, n * A + m))

        @block.gpsimd
        def _(pool):
            st.credit(pool, stored, loads[0][1](0))
            with pool.Fori(0, TILES // 2) as i:
                for j in range(2):
                    n = i * 2 + j
                    held(pool, st.marks, dv, n * V + 3 * V)
                    for dst, src in stores:
                        pool.dma_start(dst(n), src(j)).then_inc(stored[j], 16)
            for j in range(2):
                pool.wait_ge(stored[j], 16 * len(stores) * (TILES // 2) + 16)


def rope_steps(dve, step, x, cos, sin, tmp, out, halves):
    step(dve.tensor_tensor(out, x, cos, ALU.mult))
    for f in range(2):
        step(dve.tensor_tensor(halves(tmp, f), halves(x, 1 - f), halves(sin, f), ALU.mult))
    step(dve.tensor_tensor(out, out, tmp, ALU.add))


def rope_qk_norm(nc, name, qkv, heads_q, heads_k, q_gain, k_gain, cos, sin, dst):
    H = heads_q + heads_k
    W = H * HEAD
    with Stage(nc, name) as st:
        x, sq, nx, tmp, out = (st.sb(n, [P, 2, W]) for n in ("x", "sq", "nx", "tmp", "out"))
        ct, sn = st.sb("ct", [P, 2, HEAD]), st.sb("sn", [P, 2, HEAD])
        gain = st.sb("gain", [P, 2, HEAD])
        ms, inv = st.sb("ms", [P, 2, H]), st.sb("inv", [P, 2, H])
        heads = lambda v: v.rearrange("p (h w) -> p h w", w=HEAD)
        over_heads = lambda v, n: v.unsqueeze(1).to_broadcast([P, n, HEAD])

        def halves(v, f):
            return v.rearrange("p h (a f i) -> p h a f i", a=2, f=2)[:, :, :, f]

        def body(dve, step, j, wait_act):
            wait_act(1)
            step(dve.tensor_reduce(ms[:, j], heads(sq[:, j]), AX.X, ALU.add))
            step(dve.tensor_scalar(ms[:, j], ms[:, j], 1.0 / HEAD, RMS_EPS, ALU.mult, ALU.add))
            step(dve.reciprocal(inv[:, j], ms[:, j]))
            wait_act(2)
            step(dve.tensor_tensor(heads(nx[:, j]), heads(x[:, j]), ms[:, j].unsqueeze(2).to_broadcast([P, H, HEAD]), ALU.mult))
            for m, (a, b) in enumerate(((0, heads_q), (heads_q, H))):
                v = heads(nx[:, j])[:, a:b]
                step(dve.tensor_tensor(v, v, over_heads(gain[:, m], b - a), ALU.mult))
            rope_steps(dve, step, heads(nx[:, j]), over_heads(ct[:, j], H), over_heads(sn[:, j], H),
                       heads(tmp[:, j]), heads(out[:, j]), halves)

        row_stage(nc, st,
                  [(lambda j: x[:, j], lambda n: tile_at(qkv[:, 0:W], n)), (lambda j: ct[:, j], lambda n: tile_at(cos, n)),
                   (lambda j: sn[:, j], lambda n: tile_at(sin, n))],
                  [(gain[:, 0], q_gain.partition_broadcast(P)), (gain[:, 1], k_gain.partition_broadcast(P))],
                  [(lambda n: tile_at(dst, n), lambda j: out[:, j])], 10, body,
                  [(0, lambda act, j: act.activation(sq[:, j], x[:, j], ACT.Square)),
                   (3, lambda act, j: act.activation(ms[:, j], inv[:, j], ACT.Sqrt))])


def latent_norm(nc, name, proj, q_gain, kv_gain, cos, sin, cq, ckv, kr):
    RQ, RKV, RR = cq.shape[1], ckv.shape[1], kr.shape[1]
    W = RQ + RKV + RR
    parts = ((0, RQ), (RQ, RKV))
    with Stage(nc, name) as st:
        x, sq, nx = (st.sb(n, [P, 2, W]) for n in ("x", "sq", "nx"))
        tmp, out = st.sb("tmp", [P, 2, RR]), st.sb("out", [P, 2, RR])
        ct, sn = st.sb("ct", [P, 2, RR]), st.sb("sn", [P, 2, RR])
        gain = st.sb("gain", [P, RQ + RKV])
        ms, inv = st.sb("ms", [P, 2, 2]), st.sb("inv", [P, 2, 2])

        def halves(v, f):
            return v[:, f * (RR // 2):(f + 1) * (RR // 2)]

        def body(dve, step, j, wait_act):
            wait_act(1)
            for m, (a, n) in enumerate(parts):
                step(dve.tensor_reduce(ms[:, j, m:m + 1], sq[:, j, a:a + n], AX.X, ALU.add))
                step(dve.tensor_scalar(ms[:, j, m:m + 1], ms[:, j, m:m + 1], 1.0 / n, RMS_EPS, ALU.mult, ALU.add))
            step(dve.reciprocal(inv[:, j], ms[:, j]))
            wait_act(2)
            for m, (a, n) in enumerate(parts):
                step(dve.scalar_tensor_tensor(nx[:, j, a:a + n], x[:, j, a:a + n], ms[:, j, m:m + 1], gain[:, a:a + n],
                                              ALU.mult, ALU.mult))
            rope_steps(dve, step, x[:, j, RQ + RKV:W], ct[:, j], sn[:, j], tmp[:, j], out[:, j], halves)

        row_stage(nc, st,
                  [(lambda j: x[:, j], lambda n: tile_at(proj[:, 0:W], n)), (lambda j: ct[:, j], lambda n: tile_at(cos, n)),
                   (lambda j: sn[:, j], lambda n: tile_at(sin, n))],
                  [(gain[:, 0:RQ], q_gain.partition_broadcast(P)), (gain[:, RQ:], kv_gain.partition_broadcast(P))],
                  [(lambda n: tile_at(cq, n), lambda j: nx[:, j, 0:RQ]), (lambda n: tile_at(ckv, n), lambda j: nx[:, j, RQ:RQ + RKV]),
                   (lambda n: tile_at(kr, n), lambda j: out[:, j])], 11, body,
                  [(0, lambda act, j: act.activation(sq[:, j], x[:, j], ACT.Square)),
                   (5, lambda act, j: act.activation(ms[:, j], inv[:, j], ACT.Sqrt))])


def latent_heads(nc, name, q_raw, kv, kr, cos, sin, q, k, heads, nope, rr):
    W = nope + rr
    KV = kv.shape[1] // heads
    with Stage(nc, name) as st:
        x, tmp, qo, ko = st.sb("x", [P, 2, heads * W]), st.sb("tmp", [P, 2, heads * rr]), st.sb("qo", [P, 2, heads * W]), st.sb("ko", [P, 2, heads * W])
        kvt, krt = st.sb("kvt", [P, 2, heads * KV]), st.sb("krt", [P, 2, rr])
        ct, sn = st.sb("ct", [P, 2, rr]), st.sb("sn", [P, 2, rr])
        cut = lambda v, n: v.rearrange("p (h w) -> p h w", h=heads)[:, :, 0:n]
        turned = lambda v: v.rearrange("p (h w) -> p h w", h=heads)[:, :, nope:W]
        bc = lambda v: v.unsqueeze(1).to_broadcast([P, heads, rr])

        def halves(v, f):
            return v[:, :, f * (rr // 2):(f + 1) * (rr // 2)]

        def body(dve, step, j, wait_act):
            step(dve.tensor_copy(cut(qo[:, j], nope), cut(x[:, j], nope)))
            step(dve.tensor_copy(turned(ko[:, j]), bc(krt[:, j])))
            wait_act(1)
            rope_steps(dve, step, turned(x[:, j]), bc(ct[:, j]), bc(sn[:, j]),
                       tmp[:, j].rearrange("p (h w) -> p h w", h=heads), turned(qo[:, j]), halves)

        row_stage(nc, st,
                  [(lambda j: x[:, j], lambda n: tile_at(q_raw, n)), (lambda j: kvt[:, j], lambda n: tile_at(kv, n)),
                   (lambda j: krt[:, j], lambda n: tile_at(kr, n)), (lambda j: ct[:, j], lambda n: tile_at(cos, n)),
                   (lambda j: sn[:, j], lambda n: tile_at(sin, n))],
                  [], [(lambda n: tile_at(q, n), lambda j: qo[:, j]), (lambda n: tile_at(k, n), lambda j: ko[:, j])], 6, body,
                  [(1, lambda act, j: act.activation(cut(ko[:, j], nope), cut(kvt[:, j], nope), ACT.Copy))])


GDN_H = 4
GDN_W = GDN_H * HEAD
GDN_TAPS = 4


def delta_prep(nc, name, proj, first, conv_w, dst):
    W = 3 * GDN_W
    QK = 2 * GDN_H
    taps = [proj[s:s + S, first:first + W] for s in range(GDN_TAPS)]
    with Stage(nc, name) as st:
        x = st.sb("x", [P, 2, GDN_TAPS, W])
        acc, act_out, sq = (st.sb(n, [P, 2, W]) for n in ("acc", "act_out", "sq"))
        w = st.sb("w", [P, GDN_TAPS, W])
        ms, inv = st.sb("ms", [P, 2, QK]), st.sb("inv", [P, 2, QK])
        heads = lambda v: v.rearrange("p (h w) -> p h w", w=HEAD)

        def body(dve, step, j, wait_act):
            step(dve.tensor_tensor(acc[:, j], x[:, j, 0], w[:, 0], ALU.mult))
            for s in range(1, GDN_TAPS):
                step(dve.tensor_tensor(x[:, j, s], x[:, j, s], w[:, s], ALU.mult))
                step(dve.tensor_tensor(acc[:, j], acc[:, j], x[:, j, s], ALU.add))
            wait_act(2)
            step(dve.tensor_reduce(ms[:, j], heads(sq[:, j, 0:2 * GDN_W]), AX.X, ALU.add))
            step(dve.tensor_scalar(ms[:, j], ms[:, j], RMS_EPS, None, ALU.add))
            step(dve.reciprocal(inv[:, j], ms[:, j]))
            wait_act(3)
            step(dve.tensor_scalar(ms[:, j, 0:GDN_H], ms[:, j, 0:GDN_H], HEAD ** -0.5, None, ALU.mult))
            v = heads(act_out[:, j, 0:2 * GDN_W])
            step(dve.tensor_tensor(v, v, ms[:, j].unsqueeze(2).to_broadcast([P, QK, HEAD]), ALU.mult))

        def silu(act, j):
            return act.activation(act_out[:, j], acc[:, j], ACT.Silu)

        def square(act, j):
            return act.activation(sq[:, j, 0:2 * GDN_W], act_out[:, j, 0:2 * GDN_W], ACT.Square)

        row_stage(nc, st, [(lambda j, s=s: x[:, j, s], lambda n, s=s: tile_at(taps[s], n)) for s in range(GDN_TAPS)],
                  [(w[:, s], conv_w[s].partition_broadcast(P)) for s in range(GDN_TAPS)],
                  [(lambda n: tile_at(dst, n), lambda j: act_out[:, j])], 12, body,
                  [(7, silu), (7, square), (10, lambda act, j: act.activation(ms[:, j], inv[:, j], ACT.Sqrt))])


def delta_out(nc, name, o, proj, first, gain, dst):
    with Stage(nc, name) as st:
        x, z, sq, sz = (st.sb(n, [P, 2, GDN_W]) for n in ("x", "z", "sq", "sz"))
        g, ms, inv = st.sb("g", [P, HEAD]), st.sb("ms", [P, 2, GDN_H]), st.sb("inv", [P, 2, GDN_H])
        out = st.sb("out", [P, 2, GDN_W])
        heads = lambda v: v.rearrange("p (h w) -> p h w", w=HEAD)

        def body(dve, step, j, wait_act):
            wait_act(1)
            step(dve.tensor_reduce(ms[:, j], heads(sq[:, j]), AX.X, ALU.add))
            step(dve.tensor_scalar(ms[:, j], ms[:, j], 1.0 / HEAD, RMS_EPS, ALU.mult, ALU.add))
            step(dve.reciprocal(inv[:, j], ms[:, j]))
            wait_act(3)
            v = heads(out[:, j])
            step(dve.tensor_tensor(v, heads(x[:, j]), ms[:, j].unsqueeze(2).to_broadcast([P, GDN_H, HEAD]), ALU.mult))
            step(dve.tensor_tensor(v, v, g[:, :].unsqueeze(1).to_broadcast([P, GDN_H, HEAD]), ALU.mult))
            step(dve.tensor_tensor(out[:, j], out[:, j], sz[:, j], ALU.mult))

        row_stage(nc, st, [(lambda j: x[:, j], lambda n: tile_at(o, n)),
                           (lambda j: z[:, j], lambda n: tile_at(proj[:, first:first + GDN_W], n))],
                  [(g[:, :], gain.partition_broadcast(P))], [(lambda n: tile_at(dst, n), lambda j: out[:, j])], 6, body,
                  [(0, lambda act, j: act.activation(sq[:, j], x[:, j], ACT.Square)),
                   (0, lambda act, j: act.activation(sz[:, j], z[:, j], ACT.Silu)),
                   (3, lambda act, j: act.activation(ms[:, j], inv[:, j], ACT.Sqrt))])


def pool_mix(nc, name, proj, first, a, w, scale, dst):
    G, C = w.shape[0], w.shape[1]
    W = G * C
    with Stage(nc, name) as st:
        p, out = st.sb("p", [P, TILES, W]), st.sb("out", [P, TILES, W])
        band = st.sb("band", [P, 3, G, P])
        wt, sc = st.sb("wt", [C, G, C]), st.sb("sc", [P, W])
        dT = st.sb("dT", [C, 2, G, P])
        dps = [st.ps(f"dps{j}", [P, 512]) for j in range(2)]
        mps = [st.ps(f"mps{j}", [P, 512]) for j in range(2)]
        l_in, d_done, cp, m_done, scaled, stored = (st.sem(n) for n in ("l_in", "d_done", "cp", "m_done", "scaled", "stored"))
        with st.block() as block:

            @block.sync
            def _(sp):
                for dst_, src in ((p[:, :, :], rows(proj[:, first:first + W])), (band[:, :, :, :], a["pool_band"]),
                                  (wt[:, :, :], w.rearrange("g c d -> c g d")), (sc[:, :], scale.partition_broadcast(P))):
                    sp.dma_start(dst_, src).then_inc(l_in, 16)
                sp.wait_ge(scaled, TILES)
                sp.dma_start(rows(dst), out[:, :, :]).then_inc(stored, 16)
                sp.wait_ge(stored, 16)

            @block.tensor
            def _(pe):
                pe.wait_ge(l_in, 64)
                for t in range(TILES + 1):
                    if t < TILES:
                        if t >= 2:
                            pe.wait_ge(cp, t - 1)
                        for g in range(G):
                            o = dps[t % 2][0:C, g * P:(g + 1) * P]
                            last = pe.matmul(o, p[:, t, g * C:(g + 1) * C], band[:, 0 if t else 2, g], start=True, stop=t == 0)
                            if t:
                                last = pe.matmul(o, p[:, t - 1, g * C:(g + 1) * C], band[:, 1, g], start=False, stop=True)
                        last.then_inc(d_done, 1)
                    if t:
                        pe.wait_ge(cp, t)
                        if t >= 3:
                            pe.wait_ge(scaled, t - 2)
                        for g in range(G):
                            last = pe.matmul(mps[(t - 1) % 2][:, g * C:(g + 1) * C], dT[:, (t - 1) % 2, g], wt[:, g], start=True, stop=True)
                        last.then_inc(m_done, 1)

            @block.scalar
            def _(act):
                for t in range(TILES):
                    act.wait_ge(d_done, t + 1)
                    if t >= 2:
                        act.wait_ge(m_done, t - 1)
                    act.activation(dT[:, t % 2], dps[t % 2][0:C, 0:G * P].rearrange("c (g s) -> c g s", g=G), ACT.Copy).then_inc(cp, 1)

            @block.vector
            def _(dve):
                dve.wait_ge(l_in, 64)
                for t in range(TILES):
                    dve.wait_ge(m_done, t + 1)
                    dve.tensor_tensor(out[:, t], mps[t % 2][:, 0:W], sc[:, :], ALU.mult).then_inc(scaled, 1)


def delta_rule(nc, name, qkv, proj, first_ab, a_log, dt_bias, a, dst):
    H, W = GDN_H, GDN_W
    LEVELS = 6
    PE = ["turn_k_kb", "turn_q_qd", "rowbc", "at", "qkt"]
    DV = ["kb", "vb", "r", "qd", "kd", "diag", "c_k", "c_q", "lag0", "lag1", "lag2", "lag3", "decm", "at0", "at1", "qkt1", "x0", "xt0"]
    AC = ["c_kb", "c_qd", "dec", "gl"]
    for lv in range(LEVELS):
        PE += [f"t{lv}", f"x{lv}"]
        DV += [f"e{lv}"]
        AC += [f"t{lv}"]
        DV += [f"x{lv}n", f"xt{lv}n"]
    PE += ["u", "wt"]
    AC += ["u", "wt"]
    for c in range(2):
        PE += [f"ws{c}", f"o{c}", f"s{c}"]
        DV += [f"vn{c}", f"sg{c}", f"sn{c}", f"oa{c}", f"ob{c}"]
    num = {n: {tag: i + 1 for i, tag in enumerate(tags)} for n, tags in (("pe", PE), ("dv", DV), ("ac", AC))}
    NPE, NDV, NAC = len(PE), len(DV), len(AC)
    with Stage(nc, name) as st:
        sb = st.sb
        ident, ones, cm, masks = sb("ident", [P, P]), sb("ones", [P, P]), sb("cm", [P, 4, P]), sb("masks", [P, LEVELS, P])
        ab, al, dtb = sb("ab", [P, TILES, 2 * H]), sb("al", [P, H]), sb("dtb", [P, H])
        ea, pre, mag, rel, lnp, gg = sb("ea", [P, H]), sb("pre", [P, TILES, H]), sb("mag", [P, TILES, H]), sb("rel", [P, TILES, H]), sb("lnp", [P, TILES, H]), sb("gg", [P, TILES, H])
        eb, beta, gc, eg, gl_, kdf = (sb(n, [P, TILES, H]) for n in ("eb", "beta", "gc", "eg", "gl_", "kdf"))
        x = sb("x", [P, 3 * W])
        kb, vb, r, qd, kd = (sb(n, [P, W]) for n in ("kb", "vb", "r", "qd", "kd"))
        diag, dec, atT, qkT = (sb(n, [P, H, P]) for n in ("diag", "dec", "atT", "qkT"))
        kT, kbT, qT, qdT = (sb(n, [HEAD, H, P]) for n in ("kT", "kbT", "qT", "qdT"))
        e, tt, X, XT = (sb(n, [P, H, P]) for n in ("e", "tt", "X", "XT"))
        gl = sb("gl", [P, H, 2])
        u, vn, wT, state, o = sb("u", [P, H, HEAD]), sb("vn", [P, H, HEAD]), sb("wT", [HEAD, H, P]), sb("state", [HEAD, H, HEAD]), sb("o", [P, H, HEAD])
        banks = [st.ps(f"bank{n}", [P, 512]) for n in range(8)]
        l_in, x_in, su_v, su_a, su_p, pe_s, dv_s, ac_s, stored = (
            st.sem(n) for n in ("l_in", "x_in", "su_v", "su_a", "su_p", "pe_s", "dv_s", "ac_s", "stored"))
        b4 = lambda n: banks[n][:, :].rearrange("p (h s) -> p h s", h=H)
        hv = lambda v: v.rearrange("p (h w) -> p h w", h=H)
        q_, k_, v_ = (x[:, n * W:(n + 1) * W] for n in range(3))
        each = lambda v: v.unsqueeze(1).to_broadcast([P, H, P])
        UP, STRICT, CUM, SEL = range(4)

        def after(eng, sem, which, i, tag, back=0):
            n = {"pe": NPE, "dv": NDV, "ac": NAC}[which]
            eng.wait_ge(sem, i * n + (num[which][tag] + (which == "dv")))

        with st.block() as block:

            @block.sync
            def _(sp):
                for dst_, src in ((ident[:, :], a["ident"]), (ones[:, :], a["ones"]), (cm[:, :, :], a["gdn_masks"]),
                                  (masks[:, :, :], a["gdn_levels"]), (ab[:, :, :], rows(proj[GDN_TAPS - 1:, first_ab:first_ab + 2 * H])),
                                  (al[:, :], a_log.partition_broadcast(P)), (dtb[:, :], dt_bias.partition_broadcast(P))):
                    sp.dma_start(dst_, src).then_inc(l_in, 16)
                with sp.Fori(0, TILES) as i:
                    held(sp, st.marks, dv_s, i * NDV + 1)
                    sp.dma_start(x[:, :], tile_at(qkv, i)).then_inc(x_in, 16)
                    held(sp, st.marks, dv_s, i * NDV + NDV + 1)
                    sp.dma_start(tile_at(dst, i), o[:, :, :].rearrange("p h w -> p (h w)")).then_inc(stored, 16)
                sp.wait_ge(stored, 16 * TILES)

            @block.vector
            def _(dve):
                setup = steps(dve, su_v, 0)
                dve.sem_inc(dv_s, 1)
                dve.wait_ge(l_in, 16 * 7)
                bc = lambda v: v.unsqueeze(1).to_broadcast([P, TILES, H])
                setup(dve.tensor_tensor(pre[:, :, :], ab[:, :, 0:H], bc(dtb[:, :]), ALU.add))
                setup(dve.tensor_scalar(rel[:, :, :], pre[:, :, :], 0.0, None, ALU.max))
                setup(dve.scalar_tensor_tensor(mag[:, :, :], pre[:, :, :], -1.0, pre[:, :, :], ALU.mult, ALU.min))
                dve.wait_ge(su_a, 4)
                setup(dve.tensor_tensor(lnp[:, :, :], lnp[:, :, :], rel[:, :, :], ALU.add))
                setup(dve.tensor_tensor(lnp[:, :, :], lnp[:, :, :], bc(ea[:, :]), ALU.mult))
                setup(dve.tensor_scalar(gg[:, :, :], lnp[:, :, :], -1.0, None, ALU.mult))
                setup(dve.tensor_scalar(eb[:, :, :], eb[:, :, :], 1.0, None, ALU.add))
                setup(dve.reciprocal(beta[:, :, :], eb[:, :, :]))
                dve.wait_ge(su_p, 1)
                setup(dve.tensor_copy(gc[:, :, :], banks[0][:, 0:TILES * H].rearrange("p (t h) -> p t h", h=H)))
                dve.wait_ge(su_p, 2)
                setup(dve.tensor_tensor(kdf[:, :, :], banks[1][:, 0:TILES * H].rearrange("p (t h) -> p t h", h=H), gc[:, :, :], ALU.subtract))
                setup(dve.memset(state[:, :, :], 0.0))
                dve.wait_ge(su_a, 6)
                with dve.Fori(0, TILES) as i:
                    step_ = steps(dve, dv_s, i * NDV + 1)
                    done = []

                    def step(tag, ins):
                        done.append(tag)
                        assert DV[len(done) - 1] == tag, (tag, DV[len(done) - 1])
                        step_(ins)

                    def per_head(v):
                        return v[:, ds(i, 1), :].rearrange("p a h -> p (a h)").unsqueeze(2).to_broadcast([P, H, HEAD])

                    dve.wait_ge(x_in, i * 16 + 16)
                    step("kb", dve.tensor_tensor(hv(kb[:, :]), hv(k_), per_head(beta), ALU.mult))
                    step("vb", dve.tensor_tensor(hv(vb[:, :]), hv(v_), per_head(beta), ALU.mult))
                    step("r", dve.tensor_tensor(hv(r[:, :]), hv(kb[:, :]), per_head(eg), ALU.mult))
                    step("qd", dve.tensor_tensor(hv(qd[:, :]), hv(q_), per_head(eg), ALU.mult))
                    step("kd", dve.tensor_tensor(hv(kd[:, :]), hv(k_), per_head(kdf), ALU.mult))
                    gcb = gc[:, ds(i, 1), :].rearrange("p a h -> p (a h)").unsqueeze(2).to_broadcast([P, H, P])
                    step("diag", dve.tensor_tensor(diag[:, :, :], each(ident[:, :]), gcb, ALU.mult))
                    after(dve, pe_s, "pe", i, "turn_k_kb")
                    step("c_k", dve.tensor_copy(kT[:, :, :], b4(0)[0:HEAD]))
                    after(dve, pe_s, "pe", i, "turn_q_qd")
                    step("c_q", dve.tensor_copy(qT[:, :, :], b4(2)[0:HEAD]))
                    after(dve, pe_s, "pe", i, "rowbc")
                    step("lag0", dve.tensor_tensor(dec[:, :, :], b4(4), gcb, ALU.subtract))
                    step("lag1", dve.tensor_tensor(dec[:, :, :], dec[:, :, :], each(cm[:, UP]), ALU.mult))
                    step("lag2", dve.tensor_copy(X[:, :, :], each(ident[:, :])))
                    step("lag3", dve.tensor_copy(XT[:, :, :], each(ident[:, :])))
                    after(dve, ac_s, "ac", i, "dec")
                    step("decm", dve.tensor_tensor(dec[:, :, :], dec[:, :, :], each(cm[:, UP]), ALU.mult))
                    after(dve, pe_s, "pe", i, "at")
                    step("at0", dve.tensor_tensor(atT[:, :, :], b4(5), dec[:, :, :], ALU.mult))
                    step("at1", dve.tensor_tensor(atT[:, :, :], atT[:, :, :], each(cm[:, STRICT]), ALU.mult))
                    after(dve, pe_s, "pe", i, "qkt")
                    step("qkt1", dve.tensor_tensor(qkT[:, :, :], b4(6), dec[:, :, :], ALU.mult))
                    step("x0", dve.memset(vn[:, :, :], 0.0))
                    step("xt0", dve.memset(o[:, :, :], 0.0))
                    for lv in range(LEVELS):
                        step(f"e{lv}", dve.tensor_tensor(e[:, :, :], atT[:, :, :], each(masks[:, lv]), ALU.mult))
                        after(dve, pe_s, "pe", i, f"x{lv}")
                        step(f"x{lv}n", dve.tensor_tensor(X[:, :, :], X[:, :, :], b4(5), ALU.subtract))
                        step(f"xt{lv}n", dve.tensor_tensor(XT[:, :, :], XT[:, :, :], b4(6), ALU.subtract))
                    after(dve, ac_s, "ac", i, "wt")
                    for c in range(2):
                        cr = slice(c * HEAD, (c + 1) * HEAD)
                        after(dve, pe_s, "pe", i, f"ws{c}")
                        step(f"vn{c}", dve.tensor_tensor(vn[cr], u[cr], hv(banks[4][cr, 0:W]), ALU.subtract))
                        after(dve, pe_s, "pe", i, f"o{c}")
                        step(f"sg{c}", dve.tensor_tensor(state[:, :, :], state[:, :, :],
                                                         gl[0:HEAD, :, c].unsqueeze(2).to_broadcast([HEAD, H, HEAD]), ALU.mult))
                        after(dve, pe_s, "pe", i, f"s{c}")
                        step(f"sn{c}", dve.tensor_tensor(state[:, :, :], state[:, :, :], hv(banks[7][0:HEAD, 0:W]), ALU.add))
                        step(f"oa{c}", dve.tensor_copy(o[cr], hv(banks[5][cr, 0:W])))
                        step(f"ob{c}", dve.tensor_tensor(o[cr], o[cr], hv(banks[6][cr, 0:W]), ALU.add))

            @block.scalar
            def _(act):
                setup = steps(act, su_a, 0)
                act.wait_ge(l_in, 16 * 7)
                setup(act.activation(ea[:, :], al[:, :], ACT.Exp))
                setup(act.activation(eb[:, :, :], ab[:, :, H:2 * H], ACT.Exp, scale=-1.0))
                act.wait_ge(su_v, 3)
                setup(act.activation(lnp[:, :, :], mag[:, :, :], ACT.Exp))
                setup(act.activation(lnp[:, :, :], lnp[:, :, :], ACT.Ln, bias=1.0))
                act.wait_ge(su_v, 9)
                setup(act.activation(eg[:, :, :], gc[:, :, :], ACT.Exp))
                act.wait_ge(su_v, 10)
                setup(act.activation(kdf[:, :, :], kdf[:, :, :], ACT.Exp))
                with act.Fori(0, TILES) as i:
                    step_ = steps(act, ac_s, i * NAC)
                    done = []

                    def step(tag, ins):
                        done.append(tag)
                        assert AC[len(done) - 1] == tag
                        step_(ins)

                    after(act, pe_s, "pe", i, "turn_k_kb")
                    step("c_kb", act.activation(kbT[:, :, :], b4(1)[0:HEAD], ACT.Copy))
                    after(act, pe_s, "pe", i, "turn_q_qd")
                    step("c_qd", act.activation(qdT[:, :, :], b4(3)[0:HEAD], ACT.Copy))
                    after(act, dv_s, "dv", i, "lag1")
                    step("dec", act.activation(dec[:, :, :], dec[:, :, :], ACT.Exp))
                    step("gl", act.activation(gl[:, :, :], b4(4)[:, :, HEAD - 1:P:HEAD], ACT.Exp))
                    for lv in range(LEVELS):
                        after(act, pe_s, "pe", i, f"t{lv}")
                        step(f"t{lv}", act.activation(tt[:, :, :], b4(7), ACT.Copy))
                    after(act, pe_s, "pe", i, "u")
                    step("u", act.activation(u[:, :, :], hv(banks[0][:, 0:W]), ACT.Copy))
                    after(act, pe_s, "pe", i, "wt")
                    step("wt", act.activation(wT[:, :, :], b4(1)[0:HEAD], ACT.Copy))

            @block.tensor
            def _(pe):
                pe.wait_ge(l_in, 16 * 7)
                pe.wait_ge(su_v, 6)
                flat = gg[:, :, :].rearrange("p t h -> p (t h)")
                pe.matmul(banks[0][:, 0:TILES * H], cm[:, CUM], flat, start=True, stop=True).then_inc(su_p, 1)
                pe.wait_ge(su_v, 9)
                pe.matmul(banks[1][:, 0:TILES * H], cm[:, SEL], gc[:, :, :].rearrange("p t h -> p (t h)"), start=True, stop=True).then_inc(su_p, 1)
                pe.wait_ge(su_v, 11)
                with pe.Fori(0, TILES) as i:
                    done = []

                    def step(tag, ins):
                        done.append(tag)
                        assert PE[len(done) - 1] == tag
                        ins.then_inc(pe_s, 1)

                    def heads(fn):
                        for h in range(H):
                            last = fn(h)
                        return last

                    def turn(bank, src):
                        return heads(lambda h: pe.transpose(banks[bank][0:HEAD, h * P:(h + 1) * P], src[:, h * HEAD:(h + 1) * HEAD], ident[:, :]))

                    def mark():
                        pe.sem_inc(st.marks, 1)

                    after(pe, dv_s, "dv", i, "kb")
                    mark()
                    turn(0, k_)
                    step("turn_k_kb", turn(1, kb))
                    after(pe, dv_s, "dv", i, "qd")
                    mark()
                    turn(2, q_)
                    step("turn_q_qd", turn(3, qd))
                    after(pe, dv_s, "dv", i, "diag")
                    step("rowbc", pe.matmul(banks[4][:, :], ones[:, :], diag[:, :, :].rearrange("p h s -> p (h s)"), start=True, stop=True))
                    after(pe, dv_s, "dv", i, "c_k")
                    after(pe, ac_s, "ac", i, "c_kb")
                    mark()
                    step("at", heads(lambda h: pe.matmul(banks[5][:, h * P:(h + 1) * P], kT[:, h], kbT[:, h], start=True, stop=True)))
                    after(pe, dv_s, "dv", i, "c_q")
                    mark()
                    step("qkt", heads(lambda h: pe.matmul(banks[6][:, h * P:(h + 1) * P], kT[:, h], qT[:, h], start=True, stop=True)))
                    for lv in range(LEVELS):
                        after(pe, dv_s, "dv", i, f"e{lv}")
                        step(f"t{lv}", heads(lambda h: pe.matmul(banks[7][:, h * P:(h + 1) * P], e[:, h], X[:, h], start=True, stop=True)))
                        after(pe, ac_s, "ac", i, f"t{lv}")
                        heads(lambda h: pe.matmul(banks[5][:, h * P:(h + 1) * P], XT[:, h], tt[:, h], start=True, stop=True))
                        step(f"x{lv}", heads(lambda h: pe.matmul(banks[6][:, h * P:(h + 1) * P], tt[:, h], XT[:, h], start=True, stop=True)))
                    after(pe, dv_s, "dv", i, f"xt{LEVELS - 1}n")
                    step("u", heads(lambda h: pe.matmul(banks[0][:, h * HEAD:(h + 1) * HEAD], XT[:, h], vb[:, h * HEAD:(h + 1) * HEAD], start=True, stop=True)))
                    step("wt", heads(lambda h: pe.matmul(banks[1][0:HEAD, h * P:(h + 1) * P], r[:, h * HEAD:(h + 1) * HEAD], XT[:, h], start=True, stop=True)))
                    after(pe, ac_s, "ac", i, "wt")
                    for c in range(2):
                        cr = slice(c * HEAD, (c + 1) * HEAD)
                        hs = lambda h: slice(h * HEAD, (h + 1) * HEAD)
                        if c:
                            after(pe, dv_s, "dv", i, "sn0")
                        mark()
                        step(f"ws{c}", heads(lambda h: pe.matmul(banks[4][cr, hs(h)], wT[:, h, cr], state[:, h], start=True, stop=True)))
                        heads(lambda h: pe.matmul(banks[5][cr, hs(h)], qdT[:, h, cr], state[:, h], start=True, stop=True))
                        after(pe, dv_s, "dv", i, f"vn{c}")
                        mark()
                        step(f"o{c}", heads(lambda h: pe.matmul(banks[6][cr, hs(h)], qkT[cr, h, cr], vn[cr, h], start=True, stop=True)))
                        step(f"s{c}", heads(lambda h: pe.matmul(banks[7][0:HEAD, hs(h)], kd[cr, hs(h)], vn[cr, h], start=True, stop=True)))


def clear_rows(nc, name, dst):
    with Stage(nc, name) as st:
        zero = st.sb("zero", list(dst.shape))
        zeroed, stored = st.sem("zeroed"), st.sem("stored")
        with st.block() as block:

            @block.vector
            def _(dve):
                dve.memset(zero[:, :], 0.0).then_inc(zeroed, 1)

            @block.sync
            def _(sp):
                sp.wait_ge(zeroed, 1)
                sp.dma_start(dst, zero[:, :]).then_inc(stored, 16)
                sp.wait_ge(stored, 16)


def rope_tables():
    f32 = np.float32
    t = np.arange(S)
    half = HEAD // 4
    inv = f32(10000.0) ** (-np.arange(half, dtype=f32) / f32(half))
    grid = np.stack([t // GRID_W, t % GRID_W], axis=-1).astype(f32)[:, :, None] * inv
    line = t.astype(f32)[:, None] * inv[None, :]
    grid2 = np.stack([grid, grid], axis=2)
    line2 = np.stack([line, line], axis=1)
    sign = np.array([-1, 1], f32)
    return {"cos_grid": np.cos(grid2).reshape(S, HEAD), "sin_grid": (np.sin(grid2) * sign[None, None, :, None]).reshape(S, HEAD),
            "cos_line": np.cos(line2).reshape(S, 2 * half), "sin_line": (np.sin(line2) * sign[None, :, None]).reshape(S, 2 * half)}


def gdn_tables():
    j, i = np.arange(P)[:, None], np.arange(P)[None, :]
    same = j // 64 == i // 64
    masks = [same & (i >= j), same & (i > j), same & (j <= i), (j == i // 64 * 64 + 63)]
    levels = [(j // (2 * s) == i // (2 * s)) & (j // s % 2 == 0) & (i // s % 2 == 1) for s in (1, 2, 4, 8, 16, 32)]
    return {"gdn_masks": np.stack(masks, axis=1).astype(np.float32), "gdn_levels": np.stack(levels, axis=1).astype(np.float32)}


def pool_bands():
    out = np.zeros((P, 3, 4, P), np.float32)
    s, t = np.arange(P)[:, None], np.arange(P)[None, :]
    for g, win in enumerate((2, 4, 8, 16)):
        inside = (s <= t) & (s > t - win)
        out[:, 0, g] = inside / win - (s == t)
        out[:, 1, g] = (s - P > t - win) / win
        out[:, 2, g] = inside / np.minimum(t + 1, win) - (s == t)
    return out


def host_constants():
    f32 = np.float32
    part = np.arange(P)
    moe = [np.arange(N_GROUPS, 0, -1), np.arange(PER_GROUP, 0, -1), P * np.arange(TILES), np.arange(MOE_BLOCKS)]
    moe = np.concatenate([np.tile(np.concatenate(moe), (P, 1)), part[:, None]], axis=1)
    return {
        "ident": np.eye(P, dtype=f32),
        "flip": np.tile(np.eye(GRID_W, dtype=f32)[::-1], (1, 2)),
        "ones": np.ones((P, P), f32),
        "tri": (part[:, None] < part[None, :]).astype(f32),
        "moe_const": moe.astype(f32),
        **rope_tables(),
        **gdn_tables(),
        "pool_band": pool_bands(),
        "tok_id": (part[:, None] + P * np.arange(TILES)[None, :]).astype(np.uint32),
    }


def build(nc, a, out):
    def scratch(name, *shape, dt=F32):
        return nc.dram_tensor(f"sc_{name}", list(shape), dt, kind="Internal").ap()

    mod0 = scratch("mod0", 1, 6 * D)
    modulation(nc, "mod0", a["c"], a["ada_w"][0], a["ada_b"][0:1], mod0)
    pad = scratch("rpb_padded", 18, 15 * 31)
    bias = scratch("bias", 16, P, FULL_BIAS + INNER_BIAS)
    neighbour_bias(nc, "nbias", a["na_rpb"][0], pad, bias, a["flip"])
    qkv0 = scratch("qkv0", S, 3 * D)
    h0 = scratch("h0", S, D)
    modulate(nc, "h0", a["x"][0], mod0, 0, h0)
    project(nc, "qkv0", h0, a["na_w_qkv"][0], qkv0, a["ident"])
    shared = {"row_table": scratch("row_table", ROW_BLOCKS * P, 1, dt=U32), "plan": scratch("plan", 1, MOE_BLOCKS + 1, dt=U32),
              "places": scratch("places", P, 2, TILES, dt=U32), "gates": scratch("gates", P, 2, TILES),
              "logits": scratch("logits", S, N_GROUPS + N_EXPERTS), "rows": scratch("expert_rows", MOE_BLOCKS * P, D)}
    fewest = S * 2 // P
    o0 = scratch("o0", S, D)
    attention(nc, "na", (qkv0, 0, HEAD, HEAD), (qkv0, D, HEAD, HEAD), (qkv0, 2 * D, HEAD, HEAD), (o0, 0, HEAD, HEAD), a["ident"],
              groups=8, heads=2, shared=False, dk=HEAD, scale=HEAD ** -0.5, units=neighbour_units(), bias=bias, clear=shared["rows"][fewest * P:, :])
    y0 = scratch("y0", S, D)
    project(nc, "o0", o0, a["na_w_o"][0], y0, a["ident"])
    alpha = 4 ** 0.25
    x1, h1 = scratch("x1", S, D), scratch("h1", S, D)
    residual_norm(nc, "n0", a["x"][0], mod0, 2, a["ln_g"][0, 0], a["ln_b"][0, 0], alpha, x1, y=y0, nxt=(mod0, 3, h1))

    def moe(name, h, w_router, b_router, w_gate, w_up, w_down, layer):
        project(nc, name + "l", h, w_router, shared["logits"], a["ident"])
        route(nc, name + "r", shared["logits"], b_router, a, layer, shared["row_table"], shared["plan"], shared["places"], shared["gates"])
        experts(nc, name + "x", h, shared["row_table"], shared["plan"], w_gate, w_up, w_down, shared["rows"], a["ident"])
        return shared["rows"], shared["places"], shared["gates"]

    ex = moe("m0", h1, a["w_router"][0], a["b_router"][0], a["moe_w_gate"], a["moe_w_up"], a["moe_w_down"], 0)
    x2, h2 = scratch("x2", S, D), scratch("h2", S, D)
    mod1, mod2 = scratch("mod1", 1, 6 * D), scratch("mod2", 1, 6 * D)
    modulation(nc, "mod1", a["c"], a["ada_w"][1], a["ada_b"][1:2], mod1)
    modulation(nc, "mod2", a["c_2"], a["w_mod_2"][0], a["b_mod_2"][0:1], mod2)
    residual_norm(nc, "n1", x1, mod0, 5, a["ln_g"][0, 1], a["ln_b"][0, 1], alpha, x2, experts=ex, nxt=(mod1, 0, h2))

    KVH = 4
    qkv1, qk1, o1, y1 = scratch("qkv1", S, D + 2 * KVH * HEAD), scratch("qk1", S, D + KVH * HEAD), scratch("o1", S, D), scratch("y1", S, D)
    project(nc, "qkv1", h2, a["gqa_w_qkv"][0], qkv1, a["ident"])
    rope_qk_norm(nc, "rope1", qkv1, 16, KVH, a["gqa_q_norm"][0], a["gqa_k_norm"][0], a["cos_grid"], a["sin_grid"], qk1)
    attention(nc, "gqa", (qk1, 0, HEAD, HEAD), (qk1, D, HEAD, HEAD), (qkv1, D + KVH * HEAD, HEAD, HEAD), (o1, 0, HEAD, HEAD), a["ident"],
              groups=KVH, heads=16 // KVH, shared=True, dk=HEAD, scale=HEAD ** -0.5, units=[(0, S, None)] * TILES)
    project(nc, "o1", o1, a["gqa_w_o"][0], y1, a["ident"])
    x3, h3 = scratch("x3", S, D), scratch("h3", S, D)
    residual_norm(nc, "n2", x2, mod1, 2, a["ln_g"][1, 0], a["ln_b"][1, 0], alpha, x3, y=y1, nxt=(mod1, 3, h3))
    ex = moe("m1", h3, a["w_router"][1], a["b_router"][1], a["moe_w_gate"], a["moe_w_up"], a["moe_w_down"], 1)
    x4, h4 = scratch("x4", S, D), scratch("h4", S, D)
    residual_norm(nc, "n3", x3, mod1, 5, a["ln_g"][1, 1], a["ln_b"][1, 1], alpha, x4, experts=ex, nxt=(mod2, 0, h4))

    RQ, RKV, RR, MH, NOPE = 256, 128, 32, 8, 64
    AT_GDN = RQ + RKV + RR
    AT_Z = AT_GDN + 3 * GDN_W
    AT_AB = AT_Z + GDN_W
    AT_POOL = AT_AB + 2 * GDN_H
    padded = scratch("proj_padded", S + GDN_TAPS - 1, a["w_in_2"].shape[2])
    proj = padded[GDN_TAPS - 1:S + GDN_TAPS - 1, :]
    clear_rows(nc, "zrows", padded[0:GDN_TAPS - 1, :])
    project(nc, "win", h4, a["w_in_2"][0], proj, a["ident"])
    cq, ckv, kr = scratch("cq", S, RQ), scratch("ckv", S, RKV), scratch("kr", S, RR)
    latent_norm(nc, "lnorm", proj, a["mla_q_norm_2"][0], a["mla_kv_norm_2"][0], a["cos_line"], a["sin_line"], cq, ckv, kr)
    qraw, kv, q2, k2 = scratch("qraw", S, MH * (NOPE + RR)), scratch("kv", S, MH * 2 * HEAD), scratch("q2", S, MH * (NOPE + RR)), scratch("k2", S, MH * (NOPE + RR))
    project(nc, "uq", cq, a["mla_w_uq_2"][0], qraw, a["ident"])
    project(nc, "ukv", ckv, a["mla_w_ukv_2"][0], kv, a["ident"])
    latent_heads(nc, "lheads", qraw, kv, kr, a["cos_line"], a["sin_line"], q2, k2, MH, NOPE, RR)
    mix = scratch("mix", S, D)
    attention(nc, "mla", (q2, 0, NOPE + RR, NOPE + RR), (k2, 0, NOPE + RR, NOPE + RR), (kv, NOPE, 2 * HEAD, HEAD), (mix, 0, HEAD, HEAD), a["ident"],
              groups=MH // 2, heads=2, shared=False, dk=NOPE + RR, scale=(NOPE + RR) ** -0.5,
              units=[(0, (t + 1) * P, None) for t in range(TILES)], diagonal=True)
    gqkv, go = scratch("gqkv", S, 3 * GDN_W), scratch("go", S, GDN_W)
    delta_prep(nc, "dprep", padded, AT_GDN, a["gdn_conv_2"][0], gqkv)
    delta_rule(nc, "delta", gqkv, padded, AT_AB, a["gdn_a_log_2"][0], a["gdn_dt_bias_2"][0], a, go)
    delta_out(nc, "dout", go, proj, AT_Z, a["gdn_out_norm_2"][0], mix[:, MH * HEAD:MH * HEAD + GDN_W])
    pool_mix(nc, "pool", proj, AT_POOL, a, a["pool_w_2"][0], a["pool_scale_2"][0], mix[:, MH * HEAD + GDN_W:])
    y2 = scratch("y2", S, D)
    project(nc, "wout", mix, a["w_out_2"][0], y2, a["ident"])
    x5, h5 = scratch("x5", S, D), scratch("h5", S, D)
    alpha = 2 ** 0.25
    residual_norm(nc, "n4", x4, mod2, 2, a["ln1_g_2"][0], a["ln1_b_2"][0], alpha, x5, y=y2, nxt=(mod2, 3, h5))
    ex = moe("m2", h5, a["w_router_2"][0], a["b_router_2"][0], a["moe_w_gate_2"], a["moe_w_up_2"], a["moe_w_down_2"], 0)
    residual_norm(nc, "n5", x5, mod2, 5, a["ln2_g_2"][0], a["ln2_b_2"][0], alpha, out[0], experts=ex)


def kernel(**inputs):
    import concourse.bacc as bacc
    from concourse.bass_utils import run_bass_kernel_spmd

    nc = bacc.Bacc("TRN2", target_bir_lowering=False, num_devices=1)
    arrays, aps = {}, {}
    inputs["w_router"] = np.concatenate([inputs["moe_w_group"], inputs["moe_w_expert"]], axis=-1)
    inputs["b_router"] = np.concatenate([inputs["moe_b_group"], inputs["moe_b_expert"]], axis=-1)
    inputs["w_router_2"] = np.concatenate([inputs["router_w_group_2"], inputs["router_w_expert_2"]], axis=-1)
    inputs["b_router_2"] = np.concatenate([inputs["router_b_group_2"], inputs["router_b_expert_2"]], axis=-1)
    for name, value in {**inputs, **host_constants()}.items():
        value = np.ascontiguousarray(value)
        arrays["in_" + name] = value
        aps[name] = nc.dram_tensor("in_" + name, value.shape, mybir.dt.from_np(value.dtype), kind="ExternalInput").ap()
    out = nc.dram_tensor("out_0", (1, S, D), F32, kind="ExternalOutput").ap()
    build(nc, aps, out)
    r = run_bass_kernel_spmd(nc, [arrays], core_ids=[0])
    return r.results[0]["out_0"]
```
